# Optimizing a Trainium2 kernel written in Bass

```python
import jax, jax.numpy as jnp
from jax import lax
import numpy as np

D_MODEL = 1024
BATCH = 1
SEQ = 1024
DEPTH = 2
DEC_BATCH = 8
DEC_SEQ = 1
PAST_LEN = 1024
PAGE_SIZE = 128

HEAD_DIM = 64
MIX_WIDTH = D_MODEL
N_HEADS_TOTAL = MIX_WIDTH // HEAD_DIM
H_A = N_HEADS_TOTAL // 2
H_B = N_HEADS_TOTAL // 4
H_C = N_HEADS_TOTAL - H_A - H_B
KV_A = max(1, H_A // 4)
GQA_A = H_A // KV_A
W_A = H_A * HEAD_DIM
W_B = H_B * HEAD_DIM
W_C = H_C * HEAD_DIM
KVW_A = KV_A * HEAD_DIM
L_CMP = 32
L_SEL = 64
TOP_N = 8
WINDOW = 512
Q_BLOCK = 128
RET_CHUNK = 128
ROPE_THETA = 10000.0
EPS = 1e-6
ATT_SCALE = HEAD_DIM ** -0.5
RET_KEY_SCALE = HEAD_DIM ** -0.5
FORCE_BONUS = 1e3
FOX_BIAS_CENTER = 2.5
_SPLIT_SIZES = (W_A, KVW_A, KVW_A, KVW_A, KVW_A, KVW_A, KVW_A, 3 * H_A, W_A,
                W_B, W_B, W_B, H_B, W_B,
                W_C, W_C, W_C, W_C)
D_IN = sum(_SPLIT_SIZES)

kernel_name = 'hymba_nsa_fox_retention_step'

f32 = jnp.float32

def _rmsnorm(x, w):
    xf = x.astype(f32)
    y = xf * lax.rsqrt(jnp.mean(xf * xf, axis=-1, keepdims=True) + EPS)
    return (y * w.astype(f32)).astype(x.dtype)

def _rope(x, pos):
    half = HEAD_DIM // 2
    inv = ROPE_THETA ** (-jnp.arange(half, dtype=f32) / half)
    ang = pos.astype(f32)[:, None] * inv[None, :]
    cos = jnp.cos(ang)[None, :, None, :]
    sin = jnp.sin(ang)[None, :, None, :]
    xf = x.astype(f32)
    x1, x2 = xf[..., :half], xf[..., half:]
    return jnp.concatenate([x1 * cos - x2 * sin, x2 * cos + x1 * sin], axis=-1).astype(x.dtype)

def _masked_softmax(s, mask):
    s = jnp.where(mask, s.astype(f32), -jnp.inf)
    m = jnp.max(s, axis=-1, keepdims=True)
    m = jnp.where(jnp.isfinite(m), m, 0.0)
    p = jnp.where(mask, jnp.exp(s - m), 0.0)
    den = jnp.sum(p, axis=-1, keepdims=True)
    return p / jnp.where(den > 0, den, 1.0)

def _rows(a, start, n):
    return lax.dynamic_slice_in_dim(a, start, n, axis=1)

def _sweep_qblocks(fn, T):
    qb = Q_BLOCK if T % Q_BLOCK == 0 else T
    out = lax.map(lambda i: fn(i * qb, qb), jnp.arange(T // qb))
    out = jnp.moveaxis(out, 0, 1)
    return out.reshape(out.shape[0], T, *out.shape[3:])

def _gather_pages(cache, layer, page_table):
    g = cache[layer, page_table]
    return g.reshape(g.shape[0], g.shape[1] * g.shape[2], *g.shape[3:])

def _project(x, pos, norm_w, w_in, fox_bf, nsa_qn, nsa_kn, fox_qn, fox_kn):
    B, T, _ = x.shape
    z = _rmsnorm(x, norm_w) @ w_in
    points = [int(p) for p in np.cumsum(_SPLIT_SIZES)[:-1]]
    (a_q, a_kc, a_vc, a_ks, a_vs, a_kw, a_vw, a_g, a_gate,
     b_q, b_k, b_v, b_f, b_gate, c_q, c_k, c_v, c_gate) = jnp.split(z, points, axis=-1)

    def heads(t, h):
        return t.reshape(B, T, h, HEAD_DIM)

    def qk(t, h, g):
        return _rope(_rmsnorm(heads(t, h), g), pos)

    aq = qk(a_q, H_A, nsa_qn)
    akc = qk(a_kc, KV_A, nsa_kn[0])
    aks = qk(a_ks, KV_A, nsa_kn[1])
    akw = qk(a_kw, KV_A, nsa_kn[2])
    avc, avs, avw = heads(a_vc, KV_A), heads(a_vs, KV_A), heads(a_vw, KV_A)
    ag = jax.nn.sigmoid(a_g.reshape(B, T, H_A, 3))
    bq = _rmsnorm(heads(b_q, H_B), fox_qn)
    bk = _rmsnorm(heads(b_k, H_B), fox_kn)
    bv = heads(b_v, H_B)
    logf = jax.nn.log_sigmoid(b_f.astype(f32) + fox_bf.astype(f32))
    cq = _rope(heads(c_q, H_C), pos)
    ck = _rope(heads(c_k, H_C), pos) * RET_KEY_SCALE
    cv = heads(c_v, H_C)
    gate = jax.nn.silu(jnp.concatenate([a_gate, b_gate, c_gate], axis=-1))
    return (aq, akc, avc, aks, avs, akw, avw, ag, bq, bk, bv, logf, cq, ck, cv, gate)

def _nsa_compressed(q, kc, vc, q_pos):
    B, Tq = q.shape[:2]
    T = kc.shape[1]
    nb = T // L_CMP
    kb = kc[:, :nb * L_CMP].reshape(B, nb, L_CMP, KV_A, HEAD_DIM).mean(axis=2)
    vb = vc[:, :nb * L_CMP].reshape(B, nb, L_CMP, KV_A, HEAD_DIM).mean(axis=2)
    qg = q.reshape(B, Tq, KV_A, GQA_A, HEAD_DIM)
    s = jnp.einsum('btkgd,bnkd->btkgn', qg, kb) * ATT_SCALE
    blk_end = (jnp.arange(nb) + 1) * L_CMP - 1
    mask = (blk_end[None, :] <= q_pos[:, None])[None, :, None, None, :]
    p = _masked_softmax(s, mask)
    o = jnp.einsum('btkgn,bnkd->btkgd', p.astype(vb.dtype), vb)
    return o.reshape(B, Tq, H_A, HEAD_DIM), p

def _nsa_select_indices(p_cmp, q_pos, T):
    imp = p_cmp.sum(axis=3)
    nb = imp.shape[-1]
    r = L_SEL // L_CMP
    n_sel = -(-T // L_SEL)
    imp = jnp.pad(imp, ((0, 0), (0, 0), (0, 0), (0, n_sel * r - nb)))
    imp = imp.reshape(*imp.shape[:3], n_sel, r).sum(-1)
    j = jnp.arange(n_sel)
    cur = q_pos // L_SEL
    valid = j[None, :] <= cur[:, None]
    forced = (j[None, :] == 0) | (j[None, :] == cur[:, None]) | (j[None, :] == cur[:, None] - 1)
    score = jnp.where(valid[None, :, None, :], imp + jnp.where(forced, FORCE_BONUS, 0.0)[None, :, None, :], -1.0)
    _, idx = lax.top_k(score, min(TOP_N, n_sel))
    return idx

def _sel_blocks(k):
    B, T = k.shape[:2]
    n_sel = -(-T // L_SEL)
    k = jnp.pad(k, ((0, 0), (0, n_sel * L_SEL - T), (0, 0), (0, 0)))
    return k.reshape(B, n_sel, L_SEL, KV_A, HEAD_DIM).transpose(0, 3, 1, 2, 4)

def _nsa_selected(q, idx, q_pos, ksb, vsb):
    B, Tq = q.shape[:2]
    qg = q.reshape(B, Tq, KV_A, GQA_A, HEAD_DIM)
    bi = jnp.arange(B)[:, None, None, None]
    hi = jnp.arange(KV_A)[None, None, :, None]
    kg = ksb[bi, hi, idx]
    vg = vsb[bi, hi, idx]
    s = jnp.einsum('btkgd,btknld->btkgnl', qg, kg) * ATT_SCALE
    s = s.reshape(B, Tq, KV_A, GQA_A, -1)
    kpos = (idx[..., None] * L_SEL + jnp.arange(L_SEL)).reshape(B, Tq, KV_A, 1, -1)
    mask = kpos <= q_pos[None, :, None, None, None]
    p = _masked_softmax(s, mask).astype(vg.dtype)
    o = jnp.einsum('btkgs,btksd->btkgd', p, vg.reshape(B, Tq, KV_A, -1, HEAD_DIM))
    return o.reshape(B, Tq, H_A, HEAD_DIM)

def _window_attend(q, kw, vw, q_pos, k_pos):
    B, Tq = q.shape[:2]
    qg = q.reshape(B, Tq, KV_A, GQA_A, HEAD_DIM)
    s = jnp.einsum('btkgd,bskd->btkgs', qg, kw) * ATT_SCALE
    d = q_pos[:, None] - k_pos[None, :]
    mask = ((d >= 0) & (d < WINDOW) & (k_pos[None, :] >= 0))[None, :, None, None, :]
    p = _masked_softmax(s, mask).astype(vw.dtype)
    o = jnp.einsum('btkgs,bskd->btkgd', p, vw)
    return o.reshape(B, Tq, H_A, HEAD_DIM)

def _nsa_combine(ag, o_cmp, o_slc, o_win):
    return ag[..., 0:1] * o_cmp + ag[..., 1:2] * o_slc + ag[..., 2:3] * o_win

def _fox_attend(q, k, v, cq, ck, q_pos, k_pos):
    s = jnp.einsum('bthd,bshd->bhts', q, k).astype(f32) * ATT_SCALE
    s = s + jnp.moveaxis(cq, 1, 2)[..., :, None] - jnp.moveaxis(ck, 1, 2)[..., None, :]
    mask = (k_pos[None, :] <= q_pos[:, None])[None, None]
    p = _masked_softmax(s, mask).astype(v.dtype)
    return jnp.einsum('bhts,bshd->bthd', p, v)

def _retention(q, k, v, r0):
    B, T, H, D = q.shape
    c = RET_CHUNK if T % RET_CHUNK == 0 else T
    n = T // c
    log_g = jnp.log1p(-jnp.exp2(-5.0 - jnp.arange(H, dtype=f32)))
    i = jnp.arange(c, dtype=f32)
    diff = i[:, None] - i[None, :]
    dmask = jnp.where(diff >= 0, jnp.exp(jnp.maximum(diff, 0.0) * log_g[:, None, None]), 0.0)
    xi = jnp.exp((i + 1.0)[None, :] * log_g[:, None])
    zeta = jnp.exp((c - 1.0 - i)[None, :] * log_g[:, None])
    g_c = jnp.exp(c * log_g)

    def to_chunks(a):
        return jnp.moveaxis(a.astype(f32).reshape(B, n, c, H, D), 1, 0)

    def step(R, qkv):
        qc, kc, vc = qkv
        a = jnp.einsum('bihd,bjhd->bhij', qc, kc) * dmask
        o = (jnp.einsum('bhij,bjhe->bihe', a, vc)
             + jnp.einsum('bihd,bhde->bihe', qc, R) * xi.T[None, :, :, None])
        R = R * g_c[None, :, None, None] + jnp.einsum('bjhd,bjhe,hj->bhde', kc, vc, zeta)
        return R, o

    R, o = lax.scan(step, r0.astype(f32), (to_chunks(q), to_chunks(k), to_chunks(v)))
    o = jnp.moveaxis(o, 0, 1).reshape(B, T, H, D)
    return o, R

def _head_groupnorm(o, w):
    B, T, H, D = o.shape
    mu = jnp.mean(o, axis=-1, keepdims=True)
    var = jnp.mean(jnp.square(o - mu), axis=-1, keepdims=True)
    y = (o - mu) * lax.rsqrt(var + EPS)
    return y.reshape(B, T, H * D) * w.astype(f32)

def _merge(x, o_a, o_b, o_c, gate, ret_gn_w, w_out):
    B, T, _ = x.shape
    o = jnp.concatenate([o_a.reshape(B, T, W_A).astype(x.dtype),
                         o_b.reshape(B, T, W_B).astype(x.dtype),
                         _head_groupnorm(o_c, ret_gn_w).astype(x.dtype)], axis=-1)
    return x + (o * gate) @ w_out

def _layer_prompt(x, norm_w, w_in, fox_bf, nsa_qn, nsa_kn, fox_qn, fox_kn, ret_gn_w, w_out):
    B, T, _ = x.shape
    pos = jnp.arange(T, dtype=jnp.int32)
    (aq, akc, avc, aks, avs, akw, avw, ag, bq, bk, bv, logf, cq, ck, cv, gate) = _project(
        x, pos, norm_w, w_in, fox_bf, nsa_qn, nsa_kn, fox_qn, fox_kn)
    o_cmp, p_cmp = _nsa_compressed(aq, akc, avc, pos)
    idx = _nsa_select_indices(p_cmp, pos, T)
    ksb, vsb = _sel_blocks(aks), _sel_blocks(avs)

    def slc_blk(start, qb):
        return _nsa_selected(_rows(aq, start, qb), _rows(idx, start, qb), start + jnp.arange(qb), ksb, vsb)
    o_slc = _sweep_qblocks(slc_blk, T)
    kwp = jnp.pad(akw, ((0, 0), (WINDOW, 0), (0, 0), (0, 0)))
    vwp = jnp.pad(avw, ((0, 0), (WINDOW, 0), (0, 0), (0, 0)))

    def win_blk(start, qb):
        k_pos = start - WINDOW + jnp.arange(WINDOW + qb)
        return _window_attend(_rows(aq, start, qb), _rows(kwp, start, WINDOW + qb),
                              _rows(vwp, start, WINDOW + qb), start + jnp.arange(qb), k_pos)
    o_win = _sweep_qblocks(win_blk, T)
    o_a = _nsa_combine(ag, o_cmp, o_slc, o_win)
    c = lax.cumsum(logf, axis=1)

    def fox_blk(start, qb):
        return _fox_attend(_rows(bq, start, qb), bk, bv, _rows(c, start, qb), c, start + jnp.arange(qb), pos)
    o_b = _sweep_qblocks(fox_blk, T)
    r0 = jnp.zeros((B, H_C, HEAD_DIM, HEAD_DIM), f32)
    o_c, r_new = _retention(cq, ck, cv, r0)
    y = _merge(x, o_a, o_b, o_c, gate, ret_gn_w, w_out)
    wk = min(WINDOW, T)
    return y, (jnp.stack([akc, avc], axis=2), jnp.stack([aks, avs], axis=2), jnp.stack([bk, bv], axis=2),
               logf, jnp.stack([akw, avw], axis=2)[:, T - wk:], r_new.astype(x.dtype))

def _layer_sample(x, cache_cmp, cache_slc, cache_fkv, cache_flogf, win_state, ret_state, page_table, layer,
                  norm_w, w_in, fox_bf, nsa_qn, nsa_kn, fox_qn, fox_kn, ret_gn_w, w_out):
    B, T, _ = x.shape
    past = page_table.shape[1] * PAGE_SIZE
    pos = past + jnp.arange(T, dtype=jnp.int32)
    (aq, akc, avc, aks, avs, akw, avw, ag, bq, bk, bv, logf, cq, ck, cv, gate) = _project(
        x, pos, norm_w, w_in, fox_bf, nsa_qn, nsa_kn, fox_qn, fox_kn)
    cmp_past = _gather_pages(cache_cmp, layer, page_table)
    kc_all = jnp.concatenate([cmp_past[:, :, 0].astype(akc.dtype), akc], axis=1)
    vc_all = jnp.concatenate([cmp_past[:, :, 1].astype(avc.dtype), avc], axis=1)
    o_cmp, p_cmp = _nsa_compressed(aq, kc_all, vc_all, pos)
    slc_past = _gather_pages(cache_slc, layer, page_table)
    ks_all = jnp.concatenate([slc_past[:, :, 0].astype(aks.dtype), aks], axis=1)
    vs_all = jnp.concatenate([slc_past[:, :, 1].astype(avs.dtype), avs], axis=1)
    idx = _nsa_select_indices(p_cmp, pos, past + T)
    o_slc = _nsa_selected(aq, idx, pos, _sel_blocks(ks_all), _sel_blocks(vs_all))
    wk = win_state.shape[1]
    kw_all = jnp.concatenate([win_state[:, :, 0].astype(akw.dtype), akw], axis=1)
    vw_all = jnp.concatenate([win_state[:, :, 1].astype(avw.dtype), avw], axis=1)
    o_win = _window_attend(aq, kw_all, vw_all, pos, past - wk + jnp.arange(wk + T))
    o_a = _nsa_combine(ag, o_cmp, o_slc, o_win)
    fkv_past = _gather_pages(cache_fkv, layer, page_table)
    lf_past = _gather_pages(cache_flogf, layer, page_table)
    k_all = jnp.concatenate([fkv_past[:, :, 0].astype(bk.dtype), bk], axis=1)
    v_all = jnp.concatenate([fkv_past[:, :, 1].astype(bv.dtype), bv], axis=1)
    c_all = lax.cumsum(jnp.concatenate([lf_past.astype(f32), logf], axis=1), axis=1)
    o_b = _fox_attend(bq, k_all, v_all, c_all[:, past:], c_all, pos, jnp.arange(past + T))
    o_c, r_new = _retention(cq, ck, cv, ret_state)
    y = _merge(x, o_a, o_b, o_c, gate, ret_gn_w, w_out)
    return y, (jnp.stack([akc, avc], axis=2), jnp.stack([aks, avs], axis=2), jnp.stack([bk, bv], axis=2),
               logf, jnp.stack([kw_all, vw_all], axis=2)[:, T:], r_new.astype(ret_state.dtype))

def setup_inputs(seed: int = 0) -> dict:
    key = jax.random.key(seed)
    ks = jax.random.split(key, 20)
    nrm = jax.random.normal
    n_pages = PAST_LEN // PAGE_SIZE
    n_used = DEC_BATCH * n_pages
    n_phys = n_used + max(1, n_used // 4)
    w_keep = min(WINDOW, PAST_LEN)
    x_prompt = nrm(ks[0], (BATCH, SEQ, D_MODEL), f32)
    x_sample = nrm(ks[1], (DEC_BATCH, DEC_SEQ, D_MODEL), f32)
    cache_nsa_cmp = nrm(ks[2], (DEPTH, n_phys, PAGE_SIZE, 2, KV_A, HEAD_DIM), f32)
    cache_nsa_slc = nrm(ks[3], (DEPTH, n_phys, PAGE_SIZE, 2, KV_A, HEAD_DIM), f32)
    cache_fox_kv = nrm(ks[4], (DEPTH, n_phys, PAGE_SIZE, 2, H_B, HEAD_DIM), f32)
    cache_fox_logf = jax.nn.log_sigmoid(FOX_BIAS_CENTER + nrm(ks[5], (DEPTH, n_phys, PAGE_SIZE, H_B), f32))
    state_nsa_win = nrm(ks[6], (DEPTH, DEC_BATCH, w_keep, 2, KV_A, HEAD_DIM), f32)
    state_ret = nrm(ks[7], (DEPTH, DEC_BATCH, H_C, HEAD_DIM, HEAD_DIM), f32)
    page_table = jax.random.permutation(ks[8], n_phys)[:n_used].reshape(DEC_BATCH, n_pages).astype(jnp.int32)
    norm_w = 1.0 + 0.02 * nrm(ks[9], (DEPTH, D_MODEL), f32)
    w_in = nrm(ks[10], (DEPTH, D_MODEL, D_IN), f32) * (D_MODEL ** -0.5)
    fox_bf = jax.random.uniform(ks[11], (DEPTH, H_B), f32, 1.0, 4.0)
    nsa_q_norm = 1.0 + 0.02 * nrm(ks[12], (DEPTH, HEAD_DIM), f32)
    nsa_k_norm = 1.0 + 0.02 * nrm(ks[13], (DEPTH, 3, HEAD_DIM), f32)
    fox_q_norm = 1.0 + 0.02 * nrm(ks[14], (DEPTH, HEAD_DIM), f32)
    fox_k_norm = 1.0 + 0.02 * nrm(ks[15], (DEPTH, HEAD_DIM), f32)
    ret_gn_w = 1.0 + 0.02 * nrm(ks[16], (DEPTH, W_C), f32)
    w_out = nrm(ks[17], (DEPTH, MIX_WIDTH, D_MODEL), f32) * (MIX_WIDTH ** -0.5)
    return {'x_prompt': x_prompt, 'x_sample': x_sample,
            'cache_nsa_cmp': cache_nsa_cmp, 'cache_nsa_slc': cache_nsa_slc,
            'cache_fox_kv': cache_fox_kv, 'cache_fox_logf': cache_fox_logf,
            'state_nsa_win': state_nsa_win, 'state_ret': state_ret, 'page_table': page_table,
            'norm_w': norm_w, 'w_in': w_in, 'fox_bf': fox_bf, 'nsa_q_norm': nsa_q_norm,
            'nsa_k_norm': nsa_k_norm, 'fox_q_norm': fox_q_norm, 'fox_k_norm': fox_k_norm,
            'ret_gn_w': ret_gn_w, 'w_out': w_out}

def reference(x_prompt, x_sample, cache_nsa_cmp, cache_nsa_slc, cache_fox_kv, cache_fox_logf,
              state_nsa_win, state_ret, page_table, norm_w, w_in, fox_bf, nsa_q_norm, nsa_k_norm,
              fox_q_norm, fox_k_norm, ret_gn_w, w_out):
    yp, ys = x_prompt, x_sample
    p_states, s_states = [], []
    for l in range(DEPTH):
        wl = (norm_w[l], w_in[l], fox_bf[l], nsa_q_norm[l], nsa_k_norm[l], fox_q_norm[l], fox_k_norm[l],
              ret_gn_w[l], w_out[l])
        yp, ps = _layer_prompt(yp, *wl)
        ys, ss = _layer_sample(ys, cache_nsa_cmp, cache_nsa_slc, cache_fox_kv, cache_fox_logf,
                               state_nsa_win[l], state_ret[l], page_table, l, *wl)
        p_states.append(ps)
        s_states.append(ss)

    def stk(states, i):
        return jnp.stack([st[i] for st in states], axis=0)

    return (yp, ys,
            stk(p_states, 0), stk(s_states, 0),
            stk(p_states, 1), stk(s_states, 1),
            stk(p_states, 2), stk(s_states, 2),
            stk(p_states, 3), stk(s_states, 3),
            stk(p_states, 4), stk(s_states, 4),
            stk(p_states, 5), stk(s_states, 5))


_drawn_inputs = setup_inputs


def setup_inputs(seed=0):
    import zlib

    import numpy as np

    out = dict(_drawn_inputs(seed))
    spreads = {}
    factors = {'cache_nsa_cmp': 2.965,
     'nsa_q_norm': 8.0,
     'nsa_k_norm': 3.616,
     'fox_q_norm': 8.0,
     'fox_k_norm': 3.964,
     'ret_gn_w': 6.641,
     'cache_fox_logf': 3.739}
    for name, (base, spread) in spreads.items():
        noise = np.random.default_rng([zlib.crc32(name.encode()), seed]).standard_normal(out[name].shape)
        drawn = base * np.exp(spread * noise) if base else spread * noise
        out[name] = __import__('jax').numpy.asarray(drawn.astype(out[name].dtype))
    for name, factor in factors.items():
        out[name] = (out[name] * factor).astype(out[name].dtype)
    return out
```

```python
from contextlib import ExitStack

import numpy as np

import concourse.bass as bass
from concourse import mybir

F32 = mybir.dt.float32
F32R = mybir.dt.float32r
BF16 = mybir.dt.bfloat16
I32 = mybir.dt.int32
ALU = mybir.AluOpType
ACT = mybir.ActivationFunctionType
AX = mybir.AxisListType

P = 128
D = 1024
K = D // P
SEQ = 1024
T = SEQ // P
DEPTH = 2
NB = 8
PAST = 1024
PAGE = 128
NPG = PAST // PAGE
HD = 64
HA, HB, HC = 8, 4, 4
KV = 2
GQ = HA // KV
L_CMP, L_SEL, WINDOW = 32, 64, 512
NCMP = SEQ // L_CMP
NSEL = SEQ // L_SEL
WT = WINDOW // P
EPS = 1e-6
SCALE = HD ** -0.5
BIG = 1e30
MXH = 2 * P

SMALL = 3 * HA + HB
UNITS = []
for _kind, _n, _width in (("nsa", 2, 10 * HD), ("fox", 2, 6 * HD), ("ret", 2, 6 * HD), ("gate", 2, D // 2)):
    for _i in range(_n):
        UNITS.append({"kind": _kind, "i": _i, "width": _width + (SMALL if (_kind, _i) == ("nsa", 0) else 0),
                      "off": sum(u["width"] for u in UNITS)})
D_IN = sum(u["width"] for u in UNITS)
WMAX = max(u["width"] for u in UNITS)


def parts(u):
    if u["kind"] != "nsa":
        return [(0, u["width"])]
    a = u["width"] - 5 * HD
    return [(0, a), (a, u["width"])]


CONSTS = [("rope", (T, 2, HD)), ("mean", (T, NCMP)), ("keep", (T, NCMP)), ("bias", (T, NCMP)), ("sel_mul", (4, NSEL)),
          ("sel_add", (4, NSEL)), ("decay", (HC, P)), ("xi", (HC,)), ("zeta", (HC,))]
S_CONSTS = [("seq_T", (P,)), ("seq", (NB,)), ("same", (P,)), ("suffix", (P,)), ("own", (16,)), ("win0", (1,)), ("newm", (1,)),
            ("half", (1,)), ("g_ret", (1,)), ("hown", (HC,)), ("head_of", (HA,)), ("row_seq", (NB,)), ("fhead_of", (HB,)),
            ("frow_seq", (NB,)), ("forced", (NSEL + 1,)), ("idx_mul", (13,)), ("idx_add", (13,)), ("inv16", (1,))]
CONST_COLS = sum(int(np.prod(s)) for _, s in CONSTS)
S_CONST_COLS = sum(int(np.prod(s)) for _, s in S_CONSTS)
LOG_G = np.log1p(-np.exp2(-5.0 - np.arange(HC, dtype=np.float32))).astype(np.float32)
G_CHUNK = [float(x) for x in np.exp(np.float32(P) * LOG_G)]

SR = {"q": (0, HA * HD), "slc": (512, 256), "win": (768, 256), "fq": (1024, 256), "fkv": (1280, 512), "ret": (1792, 768),
      "cmp": (2560, 256)}
SR_COLS = 2816
CHUNKS = ([("cmp", c, 16) for c in range(4)] + [("slc", c, 16) for c in range(4)] + [("win", c, 16) for c in range(2)]
          + [("foxa", c, 8) for c in range(4)] + [("foxb", c, 8) for c in range(4)])

KV_IN = [16 * len(range(i, len(CHUNKS), 4)) for i in range(4)]


def shape_constants():
    f = np.float32
    half = HD // 2
    inv = (f(10000.0) ** (-np.arange(half, dtype=f) / f(half))).astype(f)
    ang = np.arange(SEQ + 1, dtype=f)[:, None] * inv[None, :]
    cos, sin = np.cos(ang).astype(f), np.sin(ang).astype(f)
    rope = np.stack([np.concatenate([cos, cos], 1), np.concatenate([-sin, sin], 1)], 1)
    by_tile = lambda a: a.reshape(T, P, *a.shape[1:]).transpose(1, 0, *range(2, a.ndim + 1))
    pos, blk, sel = np.arange(SEQ), np.arange(NCMP), np.arange(NSEL)
    mean = np.where(pos[:, None] // L_CMP == blk[None, :], f(1.0 / L_CMP), f(0))
    seen = (blk[None, :] + 1) * L_CMP - 1 <= pos[:, None]
    cur = pos[:, None] // L_SEL
    valid = sel[None, :] <= cur
    forced = (sel[None, :] == 0) | (sel[None, :] == cur) | (sel[None, :] == cur - 1)
    sel_add = np.where(valid, np.where(forced, 1e3, 0.0), -1.0)
    i = np.arange(P, dtype=f)
    diff = i[None, :] - i[:, None]
    decay = np.where(diff >= 0, np.exp(np.maximum(diff, 0)[None] * LOG_G[:, None, None]), 0).transpose(1, 0, 2)
    xi = np.exp((i + 1)[:, None] * LOG_G[None, :])
    zeta = np.exp((P - 1 - i)[:, None] * LOG_G[None, :])
    tab = {"rope": by_tile(rope[:SEQ]), "mean": by_tile(mean), "keep": by_tile(seen), "bias": by_tile(np.where(seen, 0, BIG)),
           "sel_mul": by_tile(valid)[:, 4:], "sel_add": by_tile(sel_add)[:, 4:], "decay": decay, "xi": xi, "zeta": zeta}
    consts = np.concatenate([tab[n].reshape(P, -1) for n, _ in CONSTS], 1).astype(f)
    p = np.arange(P)
    r64, r32 = p[:NB * HA], p[:NB * HB]
    eq = lambda a, b: a[:, None] == b[None, :]
    row = lambda a: np.broadcast_to(np.asarray(a, f), (P, len(a)))
    same = eq(p // 16, p // 16)
    st = {"seq_T": eq(np.arange(NB), p // 16), "seq": eq(p // 16, np.arange(NB)), "same": same,
          "suffix": -1.0 * (same & (p[:, None] >= p[None, :])), "own": eq(p % 16, np.arange(16)),
          "win0": BIG * (p[:, None] % 16 == 0), "newm": BIG * (p[:, None] % 16 != 15), "half": p[:, None] % 2,
          "g_ret": np.exp(LOG_G)[p // 4 % HC][:, None], "hown": eq(p // 4 % HC, np.arange(HC)),
          "head_of": eq(r64 % HA, np.arange(HA)), "row_seq": eq(r64 // HA, np.arange(NB)),
          "fhead_of": eq(r32 % HB, np.arange(HB)), "frow_seq": eq(r32 // HB, np.arange(NB)),
          "forced": row(np.isin(np.arange(NSEL + 1), (0, NSEL - 1, NSEL)) * 1e3),
          "idx_mul": row([4] * 4 + [8] * 8 + [1]), "idx_add": row([0, 1, 2, 3, 0, 1, 2, 3, 4, 5, 6, 7, 0]),
          "inv16": np.full((P, 1), 1 / 16)}
    s_consts = np.zeros((P, S_CONST_COLS), f)
    c = 0
    for n, shape in S_CONSTS:
        a = np.asarray(st[n], f)
        s_consts[:len(a), c:c + shape[0]] = a
        c += shape[0]
    return consts, s_consts, rope[SEQ:].reshape(1, 2, HD).astype(f)


class Step(dict):
    __getattr__ = dict.__getitem__


def y_stores(unit, r):
    if r == T:
        return {"nsa": 4, "fox": 2, "ret": 1}[unit["kind"]]
    if unit["kind"] == "nsa":
        return 3 if r >= T - WT else 2
    return 1 if unit["kind"] == "fox" else 0


def layer_plan():
    steps, count, gates = [], {}, {}
    freed = {"z": [], "t": [], "o": []}

    def sig(name, by=1):
        count[name] = count.get(name, 0) + by
        return count[name]

    def take(pool, reader=None):
        n = len(freed[pool])
        name = reader or f"{pool}_free{n % 2}"
        freed[pool].append((name, sig(name)))
        return Step(n=n, s=n % 2, before=freed[pool][n - 2] if n >= 2 else None, free=freed[pool][n],
                    up=sig(f"pe_{pool}") if pool != "o" else 0)

    def add(kind, **f):
        steps.append(Step(kind=kind, **f))
        return steps[-1]

    xt = []
    for r in range(T + 2):
        if r <= T:
            add("x", r=r, sq=sig("x_sq"), rs=sig("x_rs"), xn=sig("xn_ready"),
                pe=xt[r - 2].t[-1].up if r >= 2 else 0)
        if r >= 1:
            xt.append(add("xt", r=r - 1, t=[take("t") for _ in range(2 if r <= T else 1)]))
            xt[-1].update(hi=[sig("split_hi") for _ in xt[-1].t])
    slices = 0
    tiles = 0
    for u, unit in enumerate(UNITS):
        kind = unit["kind"]
        first = slices
        if kind == "fox":
            add("crow", i=unit["i"], wait_f=count["att_done"])
        for k in range(K):
            add("w", u=u, k=k, n=slices, up=sig("w_split"), wait_z=count.get("pe_z", 0), wait_f=count.get("att_done", 0))
            slices += 1
        if (kind, unit["i"]) == ("fox", 0):
            logf = add("logf", a=sig("lf_abs"), b=sig("lf_ln"), c=sig("lf_ready"), t=[take("t") for _ in range(2)],
                       scan=sig("lf_scan"))
            steps.remove(logf)
            steps.insert([s.kind for s in steps].index("crow"), logf)
        if kind == "nsa":
            mean = take("o")
        zs, ys, ros, ras = {}, {}, {}, {}
        for r in range(T + 4):
            if r <= T:
                if kind == "gate":
                    z = take("z")
                    zs[r] = add("z", u=u, r=r, z=z, slices=first, e=sig("gate_e"), xt=None)
                    gates[r] = z["free"]
                else:
                    z = take("z")
                    zs[r] = add("z", u=u, r=r, z=z, slices=first, m=tiles, b=tiles % 2, xt=xt[r].t[-1].free if u == 0 else None,
                                y_out=count.get(f"y_out{tiles % 2}", 0), y=count.get("y_ready", 0) if r == 0 else 0,
                                wait_t=0, tiles=tiles)
                    if kind != "ret":
                        zs[r].update(ysq=sig("y_in"), ss=sig("ss"), rs=sig("rs"))
                    tiles += 1
                    if y_stores(unit, r):
                        sig(f"y_out{zs[r].b}", 16 * y_stores(unit, r))
            if kind == "gate":
                continue
            if kind == "ret" and 4 <= r <= T + 3:
                add("gn", u=u, r=r - 4, rs=count["gn_rs"], up=sig("gn_out"))
            if kind == "ret" and 3 <= r <= T + 2:
                q = r - 3
                ros[q] = add("ro", u=u, r=q, at=ras[q].o.free, prev=ros[q - 1].o.free if q else None, o=take("o"), up=sig("pe_o"),
                             c=sig("ret_copy"), q=sig("gn_sq"), rs=sig("gn_rs"), gn=count.get("gn_out", 0), b=zs[q].b)
            if 1 <= r <= T + 1:
                ys[r - 1] = add("y", u=u, r=r - 1, z=zs[r - 1], up=sig("y_ready"), wait_t=count["pe_t"], wait_o=count.get("pe_o", 0))
            if 2 <= r <= T + 1:
                tr = add("tr", u=u, r=r - 2, b=zs[r - 2].b, y=ys[r - 2].up, t=[take("t") for _ in range(1 if kind == "ret" else 2)],
                         mean=mean if kind == "nsa" else None)
                if r <= T:
                    zs[r]["wait_t"] = tr.t[0].up if kind != "fox" else 0
                else:
                    last_tr = tr
                if kind == "ret":
                    ras[r - 2] = add("ra", u=u, r=r - 2, tr=tr.t[0].free, o=take("o"), up=sig("pe_o"))
        zs[0]["wait_t"] = zs[1]["wait_t"] = 0
        if kind == "nsa":
            add("kb", u=u, mean=mean, pe=last_tr.t[0].up, ready=sig("kb_split"), t=take("t"), ag=sig("ag_exp") if u == 0 else 0)
        if kind in ("nsa", "fox"):
            attend(add, sig, take, unit, u, count)
        if kind == "ret":
            add("ret_state", u=u, o=ros[T - 1].o.free)
        if (kind, unit["i"]) == ("ret", 1):
            sample_plan(add, sig, take, count)
    for k in range(K):
        add("w", u=len(UNITS), k=k, n=slices, up=sig("w_split"), wait_z=count["pe_z"], wait_f=0)
        slices += 1
    gate_z = count["pe_z"]
    mts, outs = [], []
    for r in range(T + 2):
        if r <= T:
            mts.append(add("mt", r=r, g=gates[r], wait_z=outs[r - 2].z.up if r >= 2 else gate_z,
                           t=[take("t") for _ in range(2 if r < T else 1)]))
            mts[-1].update(hi=[sig("split_hi") for _ in mts[-1].t])
        if r >= 1:
            outs.append(add("out", r=r - 1, mt=mts[r - 1].t[-1].free, slices=slices, z=take("z")))
    return steps, count


def loads_first(steps):
    held = [s for s in steps if s.kind == "w" and s.k < 3 and s.u not in (0, len(UNITS) - 2)]
    out = []
    for s in steps:
        if s not in held:
            out.append(s)
        if s.kind == "z" and s.r == 0:
            out += [h for h in held if h.u == s.u + 1]
    return out


def attend(add, sig, take, unit, u, count):
    items = []
    if unit["kind"] == "nsa":
        for t in range(T):
            for br in ("cmp", "win", "slc"):
                k0 = max(0, t - WT) if br == "win" else 0
                items.append(Step(br=br, t=t, k0=k0, lanes=[(a, t) for a in range(GQ)]))
    else:
        for h in range(2):
            for j in range(T // 4):
                items.append(Step(br="fox", h=h, t=4 * j, k0=0, lanes=[(h, 4 * j + a) for a in range(4)]))
    back = {}
    for i in range(len(items) + 2):
        front = []
        if i < len(items):
            it = items[i]
            it.update(i=i, u=u, buf=i % 2, den=i % 4, prev=items[i - 1] if i else None,
                      t_before=items[i - 2]["t_up"] if i >= 2 else 0, ot_before=items[i - 4]["ot_up"] if i >= 4 else 0,
                      c_before=items[i - 6]["t_up"] if i >= 6 else 0)
            if it.br in ("cmp", "fox"):
                sig("acc_uses")
            it.update(acc=count["acc_uses"] - 1)
            if it.br == "cmp":
                front.append(("SC", it, 0))
            else:
                front += [("S", it, a) for a in range(4)]
            last = 0 if it.br == "cmp" else it.t + (3 if it.br == "fox" else 0)
            work = []
            for kb in range(it.k0 if it.br != "cmp" else 0, last + 1):
                work.append(("T", it, kb))
                if kb > it.k0:
                    work.append(("PV", it, kb - 1))
            work.append(("PV", it, last))
            work.append(("OE", it, 0))
            back[i] = work
        behind = ([("OT", items[i - 2], 0)] if 0 <= i - 2 < len(items) else []) + back.pop(i - 1, [])
        n = max(1, len(front))
        for f in range(n):
            if front:
                emit(add, sig, take, *front[f])
            for b in behind[f * len(behind) // n:(f + 1) * len(behind) // n]:
                emit(add, sig, take, *b)


def emit(add, sig, take, what, it, x):
    last = 0 if it.br == "cmp" else it.t + (3 if it.br == "fox" else 0)
    if what == "SC":
        st = add("SC", it=it, z=take("z"), cs=sig("cmp_in"), e=sig("cmp_exp"), p=sig("cmp_p"))
        it["p_done"] = ("cmp_p", st.p)
    elif what == "S":
        masked = (it.br == "slc" and it.t >= 4) or it.br == "fox"
        z = take("z", None if masked else "p_ready")
        p = sig("p_ready") if masked else z["free"][1]
        add("S", it=it, a=x, z=z, masked=masked, nm=0 if masked else sig("nm_ready"), p=p)
        it["p_done"] = ("p_ready", p)
    elif what == "T":
        lanes = [a for a in range(4) if it.br != "fox" or it.lanes[a][1] >= x]
        st = add("T", it=it, kb=x, lanes=lanes, t=take("t"), hi=sig("pt_hi"))
        it["t_up"] = st.t.up
        it[("T", x)] = st
    elif what == "PV":
        if x == it.k0:
            it["o"] = take("o")
        st = it[("T", x)]
        it["pv"] = sig("pv_done")
        add("PV", it=it, kb=x, lanes=st.lanes, t=st.t, pt=st.hi, first=x == it.k0, last=x == last)
    elif what == "OE":
        add("OE", it=it, pv=it["pv"], ot=it.prev["ot_t"] if it.prev else 0)
    elif what == "OT":
        st = add("OT", it=it, t=take("t"), up=sig("att_done"))
        it["ot_up"], it["ot_t"] = st.up, st.t.up


def sample_plan(add, sig, take, count):
    add("s_begin", up=sig("s_begin"), pe_t=count["pe_t"], pe_z=count["pe_z"], pe_o=count["pe_o"])
    for src, c, width in (("q", 0, 512), ("new", 512, 512), ("fq", 1024, 256), ("newf", 1280, 512), ("ret", 1792, 512),
                      ("ret", 2304, 256)):
        add("s_rep", dst=src, c=c, width=width, off=512 if c == 2304 else 0, z=take("z"))
    add("s_decay", tot=sig("s_dve"), t=take("t"))
    n = 0
    for c in range(4):
        add("s_mean", c=c, n=n, up=sig("kv_used"))
        n += 1
    for br, tok, chunks in (("cmp", 2, 1), ("slc", 16, 4), ("win", 16, 2), ("foxa", 8, 4), ("foxb", 8, 4)):
        first, fox = n, br.startswith("fox")
        has_new = br in ("slc", "win", "foxb")
        for c in range(chunks):
            add("s_k", br=br, c=c, tok=tok, n=first + c if br != "cmp" else None)
        add("s_soft", br=br, toks=tok * chunks + has_new, new=has_new, nm=sig("s_dve"), t1=take("t"), nx=sig("s_dve"),
            t2=take("t"), e_in=sig("s_dve"), e=sig("s_act"), dn=sig("s_dve"), t3=take("t"))
        if br == "cmp":
            add("s_select", a=sig("s_dve"), t1=take("t"), b=sig("s_dve"), t2=take("t"))
        o = take("o")
        for c in range(chunks + has_new):
            new = c == chunks
            add("s_v", br=br, c=c, new=new, tok=1 if new else tok, n=first + c if br != "cmp" and not new else None, o=o,
                px=sig("px_ready"), up=sig("sv_done"), first=c == 0, last=c == chunks + has_new - 1)
        if br != "cmp":
            n += chunks
        if br == "foxa":
            add("s_keep", o=o)
        else:
            add("s_o", br=br, o=o, ta=[take("t"), take("t")] if fox else None, ca=[sig("s_dve"), sig("s_dve")] if fox else None,
                spread=sig("s_dve"), z=take("z"))
    add("s_ret", part=sig("s_dve"), z=take("z"), q=sig("s_dve"), rs=sig("s_pool"), end=sig("s_dve"))


def decoder_step(nc, x_prompt, x_sample, cache_cmp, cache_slc, cache_fox, cache_logf, state_win, state_ret,
                 page_table, w_in, w_out, norm_w, w7_in, w4_in, gn_w, fox_bf, consts, s_consts, rope_new,
                 y_prompt, y_sample, cmp_p, cmp_s, slc_p, slc_s, fox_p, fox_s, logf_p, logf_s, win_p, win_s,
                 ret_p, ret_s):
    steps, total = layer_plan()
    N_PHYS = cache_cmp.shape[1]
    sp_steps = loads_first(steps)
    dram = lambda name, shape, dt=F32: nc.dram_tensor(name, shape, dt, kind="Internal").ap()
    mix_d = dram("mix_rows", [SEQ, D])
    s_rows_d = dram("sampled_rows", [NB, SR_COLS])
    c_d = dram("decay_sums", [HB, SEQ])
    pages_d = dram("half_pages", [NB * NPG, 2], I32)

    with ExitStack() as ctx:
        names = set(total) | {"act_step", "dve_step", "pool_step", "ends", "next_layer", "start", "consts_in", "pages_in",
                              "c_out", "c_in", "lf_in", "r_in", "ret_st", "s_store", "lf_st", "norm_in", "row_w_in",
                              "win_shift", "ident_up", "pro_dve", "pro_pool", "pe_s", "s_end", "s_rows_in", "copied", "w_hi", "s_fox", "s_foxe", "s_state"}
        names |= {f"{p}{i}" for p in ("z_free", "t_free", "o_free", "x_in", "w_in", "y_out", "mix_out", "mix_in", "res_in",
                                      "row_out", "mx_out") for i in range(3)}
        names |= {f"kv_in{i}" for i in range(4)}
        S = {name: ctx.enter_context(nc.semaphore(name)) for name in sorted(names)}
        fired = {}

        def hit(ins, name, by=1):
            fired[name] = fired.get(name, 0) + by
            ins.then_inc(S[name], by)
            return fired[name]

        base = -(-nc.sbuf_base // 64) * 64

        def place(at, name, shape, dt=F32):
            size = int(np.prod(shape[1:])) * (2 if dt == BF16 else 4)
            size = -(-size // 32) * 32
            return nc.alloc_sbuf_tensor_at(name, shape, dt, offset=at), at + size

        at = base
        big_hi, at = place(at, "big_hi", [P, K, 1024], F32R)
        big_lo, at = place(at, "big_lo", [P, K, 1024], F32R)
        raw_at = at
        raw, at = place(at, "w_raw", [P, 3, 1024])
        region = at
        Y, at = place(at, "head_rows", [P, 2, 10 * HD])
        sq, at = place(at, "squares", [P, 7 * HD])
        rot, at = place(at, "rotated", [P, 7 * HD])
        split, at = place(at, "split_rows", [P, 2, 1024])
        post_end = at
        unit_at = at
        qT, at = place(at, "qT", [P, 4, SEQ], F32R)
        kT, at = place(at, "kT", [P, 4, SEQ], F32R)
        V, at = place(at, "V", [P, T, 2, P], F32R)
        w_at = at
        w_hi, at = place(at, "w_hi_t", [P, K, WMAX], F32R)
        w_lo, at = place(at, "w_lo_t", [P, K, WMAX], F32R)
        w_end = at
        at2 = w_at
        prob, at2 = place(at2, "prob", [P, 2, 4, SEQ])
        pt_hi, at2 = place(at2, "pt_hi_t", [P, 2, 512], F32R)
        pt_lo, at2 = place(at2, "pt_lo_t", [P, 2, 512], F32R)
        oT, at2 = place(at2, "oT", [P, 512])
        at = max(at, at2)
        at2 = region
        fin, at2 = place(at2, "fin", [P, 4, P])
        cmp_s0, at2 = place(at2, "cmp_scores", [P, 4, NCMP])
        cmp_pr, at2 = place(at2, "cmp_probs", [P, 2, 4, NCMP])
        imp4, at2 = place(at2, "imp4", [P, 4, NSEL])
        assert at2 <= post_end
        at2 = post_end - 8192
        lfT, at2 = place(at2, "logf_T", [HB, SEQ])
        cT, at2 = place(at2, "decay_T", [HB, SEQ])
        at2 = unit_at
        x_t, at2 = place(at2, "x_tile", [P, 2, D])
        xn, at2 = place(at2, "xn_tile", [P, 2, D])
        x_sq, at2 = place(at2, "x_squares", [P, D])
        norm_row, at2 = place(at2, "norm_row", [P, D])
        at2 = unit_at
        rk_T, at2 = place(at2, "ret_kT", [P, P])
        rqx_T, at2 = place(at2, "ret_qxT", [P, P])
        rq_z, at2 = place(at2, "ret_q_blocks", [P, 2, P])
        rat, at2 = place(at2, "ret_scores", [P, 2, P])
        rk, at2 = place(at2, "ret_k", [P, 2, P])
        rvz, at2 = place(at2, "ret_v_blocks", [P, 2, 2, P])
        rzv, at2 = place(at2, "ret_zeta_v", [P, 2, P])
        rstate, at2 = place(at2, "ret_state", [P, P])
        ro, at2 = place(at2, "ret_out", [P, 2, P])
        ro_sq, at2 = place(at2, "ret_squares", [P, P])
        rqx, at2 = place(at2, "ret_qx", [P, 2, P])
        ret_mix, at2 = place(at2, "ret_mix", [P, 2, P])
        assert at2 <= w_at
        gated, at2 = place(unit_at, "gated", [P, T, D])
        at2 = region
        ge, at2 = place(at2, "gate_e", [P, 2, 512])
        mixl, at2 = place(at2, "mix_tile", [P, 2, 512])
        gated_s, gates_end = place(at2, "gated_s", [NB, D])
        at2 = w_at
        mt_hi, at2 = place(at2, "mix_hi", [P, 2, K, P], F32R)
        mt_lo, at2 = place(at2, "mix_lo", [P, 2, K, P], F32R)
        res, at2 = place(at2, "residual", [P, 2, D])
        assert at2 <= w_end
        at2 = region
        kv, at2 = place(unit_at, "kv_chunks", [P, 4, 4096])
        ssc, at2 = place(at2, "s_scores", [P, 65, 8])
        cl, at2 = place(at2, "s_decay", [P, 65, HB])
        lf_t, at2 = place(at2, "s_logf", [P, 64, HB])
        RR, at2 = place(at2, "s_ret_rows", [P, 3, 256])
        kbm, at2 = place(at2, "s_block_means", [P, 2, 256])
        nmx, at2 = place(at2, "s_min_spread", [8, 8, 16])
        vp, at2 = place(at2, "s_vp", [P, HD])
        sm, at2 = place(at2, "s_small", [P, 224])
        assert at2 <= at, (at2, at)
        at2 = raw_at
        SRt, _ = place(at2, "s_rows", [NB, SR_COLS])
        pr, at2 = place(at2, "s_products", [P, 4096])
        QR, at2 = place(at2, "s_q", [P, 512])
        FQ, at2 = place(at2, "s_fq", [P, 256])
        NK, at2 = place(at2, "s_new", [P, 2, 256])
        NF, at2 = place(at2, "s_newf", [P, 512])
        assert at2 <= gates_end
        mixs, at2 = place(gates_end, "mix_s", [NB, D])
        assert at2 <= post_end
        at2 = unit_at
        s_R, at2 = place(at2, "s_state", [P, 16, HD])
        s_t1, at2 = place(at2, "s_state_q", [P, 16, HD])
        s_t2, at2 = place(at2, "s_outer", [P, 16, HD])

        def keep(name, shape, dt=F32):
            nonlocal at
            t, at = place(at, name, shape, dt)
            return t

        def columns(tensor, table):
            out, c = {}, 0
            for name, shape in table:
                n = int(np.prod(shape))
                v = tensor[:, c:c + n]
                if len(shape) == 2:
                    v = v.rearrange("p (a b) -> p a b", b=shape[1])
                if len(shape) == 3:
                    v = v.rearrange("p (a b c) -> p a b c", b=shape[1], c=shape[2])
                out[name] = v
                c += n
            return out

        cst = keep("consts_t", [P, CONST_COLS])
        C = columns(cst, CONSTS)
        scst = keep("s_consts_t", [P, S_CONST_COLS])
        SC = columns(scst, S_CONSTS)
        ident = keep("ident", [P, P])
        ident_b = keep("ident_b", [P, P], BF16)
        late_b = keep("late_b", [P, P], BF16)
        early_b = keep("early_b", [P, P], BF16)
        rope_s = keep("rope_s", [P, 2, HD])
        w7 = keep("w7", [P, 7 * HD])
        w4 = keep("w4", [P, 4 * HD])
        gn_row = keep("gn_row", [P, HC * HD])
        bf_row = keep("bf_row", [P, HB])
        small = keep("small", [P, T + 1, SMALL])
        ag = keep("ag", [P, T + 1, 3 * HA])
        xs_hi = keep("xs_hi", [P, K, NB], F32R)
        xs_lo = keep("xs_lo", [P, K, NB], F32R)
        bm = keep("bm", [P, T, NSEL])
        acc = keep("acc", [P, 2, 256])
        kvm = keep("kv_means", [NCMP, P])
        kbr = keep("k_means_rows", [NCMP, 256])
        vb = keep("vb", [NCMP, P], F32R)
        kbT = keep("kbT", [P, 2, NCMP], F32R)
        tiny = keep("tiny", [P, 208])
        TN = columns(tiny, [("ss", (2, 8)), ("rs", (2, 8)), ("halfneg", (8,)), ("nm", (8,)), ("den", (4, 4)), ("cden", (4,)),
                            ("cnm", (4,)), ("co", (4,)), ("m8", (8,)), ("imp", (NSEL + 1,)), ("rep", (NSEL + 1,)), ("one", (1,)),
                            ("xss", (2,)), ("xrs", (2,)), ("mu", (2, 2)), ("gss", (2, 2)), ("grs", (2, 2)), ("ptmp", (8,))])
        lf = keep("lf", [P, 2, T + 1, HB])
        crow = keep("crow", [P, 2, SEQ])
        at2 = at - 2 * SEQ * 4
        pw, at2 = place(at2, "s_probs_spread", [P, 1024])
        orow, at2 = place(at2, "s_out_rows", [64, 256])
        wrow, at2 = place(at2, "s_out_spread", [64, 512])
        OA, at2 = place(at2, "s_foxa", [32, 256])
        SM = columns(sm, [("nm", (8,)), ("NM", (8,)), ("dn", (8,)), ("rd", (8,)), ("NMA", (4,)), ("denA", (4,)), ("imp", (2,)),
                          ("bms", (2,)), ("fa", (4,)), ("fb", (4,)), ("coa", (1,)), ("cob", (1,)), ("mu", (4,)), ("ss", (4,)),
                          ("rs", (4,)), ("qp", (16,)), ("kp", (16,)), ("nf", (4,)), ("m8", (8,)), ("rep", (NSEL + 1,)),
                          ("sc", (2, NSEL + 1)), ("ns", (2, NSEL)), ("nmb", (8,)), ("tmp4", (8,))])
        base_f = keep("idx_base", [P, 1])
        idx_f = keep("idx_f", [P, 13])
        idx_u = keep("idx_u", [P, 13, 1], mybir.dt.uint32)
        pages = keep("pages", [P, 1], I32)
        assert at <= nc.sbuf_usable_end, (at, nc.sbuf_usable_end)

        zS = ctx.enter_context(nc.psum_tensor("z_slots", [P, 2, 2, 512], F32))
        tS = ctx.enter_context(nc.psum_tensor("t_slots", [P, 2, 512], F32))
        oS = ctx.enter_context(nc.psum_tensor("o_slots", [P, 2, 512], F32))

        def rows(r):
            return P if r < T else NB

        def wait(e, pair):
            if pair and pair[1]:
                e.wait_ge(S[pair[0]], pair[1])

        def heads(t, n=HD):
            return t.rearrange("p (h d) -> p h d", d=n)

        def bc(ap, axis, n):
            s = list(ap.unsqueeze(axis).shape)
            s[axis] = n
            return ap.unsqueeze(axis).to_broadcast(s)

        def s_gather_wait(n):
            if n < 4:
                return None
            prev = n - 4
            if CHUNKS[prev][0] == "cmp":
                return ("kv_used", prev + 1)
            return ("sv_done", [s.up for s in steps if s.kind == "s_v" and s.n == prev][0])

        kb_free = {s.u: s.t.free for s in steps if s.kind == "kb"}
        tr_free = {s.u: s.t[-1].free for s in steps if s.kind == "tr"}
        sv_before, prev_so = {}, {}
        sv_count = so_count = 0
        for st in steps:
            if st.kind == "s_v":
                sv_count = st.up
            if st.kind in ("s_o", "s_keep"):
                sv_before[id(st)] = sv_count
            if st.kind == "s_o":
                prev_so[id(st)] = so_count
                so_count = st.spread

        last_reps = [s.z.free for s in steps if s.kind == "s_rep"]

        def ssc_of(st):
            H = HB if st.br.startswith("fox") else HA
            return ssc[:].rearrange("p t h -> p (t h)")[:, 0:st.toks * H].rearrange("p (t h) -> p t h", h=H)

        block = ctx.enter_context(nc.Block())

        @block.tensor
        def _(pe):
            pe.wait_ge(S["start"], 2)

            def three(out, hi, lo, w_h, w_l, start, stop):
                pe.matmul(out, lo, w_h, start=start, stop=False)
                pe.matmul(out, hi, w_l, start=False, stop=False)
                return pe.matmul(out, hi, w_h, start=False, stop=stop)

            def project(st):
                r, z, s = st.r, st.z, st.z.s
                unit = UNITS[st.u]
                wait(pe, z.before)
                if st.xt:
                    wait(pe, st.xt)
                for k in range(K):
                    if r == 0:
                        pe.wait_ge(S["w_split"], st.slices + k + 1)
                    hi, lo = ((big_hi[:, k, r * P:(r + 1) * P], big_lo[:, k, r * P:(r + 1) * P]) if r < T
                              else (xs_hi[:, k, :], xs_lo[:, k, :]))
                    for b, (c0, c1) in enumerate(parts(unit)):
                        m = three(zS[0:rows(r), s, b, 0:c1 - c0], hi, lo, w_hi[:, k, c0:c1], w_lo[:, k, c0:c1], k == 0, k == K - 1)
                hit(m, "pe_z")

            with pe.Fori(0, DEPTH) as l:
                for st in steps:
                    kd = st.kind
                    if kd in ("xt", "mt"):
                        r = st.r
                        if kd == "xt":
                            pe.wait_ge(S["xn_ready"], r + 1)
                            src = xn[0:rows(r), r % 2, :]
                        else:
                            wait(pe, st.g)
                            src = gated[:, r, :] if r < T else gated_s[:, :]
                        for i, t in enumerate(st.t):
                            wait(pe, t.before)
                            ks = range(4 * i, 4 * i + 4) if r < T else range(K)
                            for j, k in enumerate(ks):
                                n = rows(r)
                                m = pe.transpose(tS[:, t.s, j * n:(j + 1) * n], src[:, k * P:(k + 1) * P], ident[0:n, 0:n])
                            hit(m, "pe_t")
                    elif kd == "z":
                        project(st)
                    elif kd == "out":
                        r, z = st.r, st.z
                        wait(pe, z.before)
                        wait(pe, st.mt)
                        if r == 0:
                            pe.wait_ge(S["w_split"], st.slices)
                        for k in range(K):
                            hi, lo = (mt_hi[:, r % 2, k, :], mt_lo[:, r % 2, k, :]) if r < T else (xs_hi[:, k, :], xs_lo[:, k, :])
                            for b in range(2):
                                m = three(zS[0:rows(r), z.s, b, :], hi, lo, big_hi[:, k, b * 512:(b + 1) * 512],
                                          big_lo[:, k, b * 512:(b + 1) * 512], k == 0, k == K - 1)
                        hit(m, "pe_z")
                    elif kd == "tr":
                        r, b = st.r, st.b
                        pe.wait_ge(S["y_ready"], st.y)
                        unit = UNITS[st.u]
                        if st.mean:
                            if r == 0:
                                wait(pe, st.mean.before)
                            pe.matmul(oS[0:NCMP, st.mean.s, 0:P], C["mean"][:, r, :], Y[:, b, 384:512], start=r == 0, stop=r == T - 1)
                        wait(pe, st.t[0].before)
                        if unit["kind"] == "ret":
                            for j, src in enumerate((Y[:, b, 0:P], rqx[:, b, :], rk[:, b, :])):
                                m = pe.transpose(tS[:, st.t[0].s, j * P:(j + 1) * P], src, ident[:])
                            hit(m, "pe_t")
                        else:
                            for j in range(4 if unit["kind"] == "nsa" else 2):
                                m = pe.transpose(tS[:, st.t[0].s, j * P:(j + 1) * P], split[:, b, j * P:(j + 1) * P], ident[:])
                            hit(m, "pe_t")
                            wait(pe, st.t[1].before)
                            for j in range(4):
                                m = pe.transpose(tS[:, st.t[1].s, j * P:(j + 1) * P], split[:, b, 512 + j * P:512 + (j + 1) * P], ident[:])
                            hit(m, "pe_t")
                    elif kd == "kb":
                        pe.wait_ge(S["kb_split"], st.ready)
                        wait(pe, st.t.before)
                        for j in range(2):
                            m = pe.transpose(tS[:, st.t.s, j * NCMP:(j + 1) * NCMP], kbr[:, j * P:(j + 1) * P], ident[0:NCMP, 0:NCMP])
                        hit(m, "pe_t")
                    elif kd == "logf":
                        pe.wait_ge(S["lf_ready"], st.c)
                        for i, t in enumerate(st.t):
                            wait(pe, t.before)
                            for j in range(4):
                                m = pe.transpose(tS[0:HB, t.s, j * P:(j + 1) * P], lf[:, 0, 4 * i + j, :], ident[:])
                            hit(m, "pe_t")
                    elif kd == "ra":
                        wait(pe, st.o.before)
                        wait(pe, st.tr)
                        hit(pe.matmul(oS[:, st.o.s, 0:256], rk_T[:], rq_z[:].rearrange("p h n -> p (h n)"), start=True, stop=True), "pe_o")
                    elif kd == "ro":
                        b = st.b
                        wait(pe, st.o.before)
                        wait(pe, st.at)
                        wait(pe, st.prev)
                        for h in range(2):
                            pe.matmul(oS[:, st.o.s, 0:P], rat[:, h, :], rvz[:, b, h, :], start=h == 0, stop=False)
                        pe.matmul(oS[:, st.o.s, 0:P], rqx_T[:], rstate[:], start=False, stop=True)
                        hit(pe.matmul(oS[:, st.o.s, P:2 * P], rk[:, b, :], rzv[:, b, :], start=True, stop=True), "pe_o")
                    elif kd == "SC":
                        it = st.it
                        wait(pe, st.z.before)
                        if it.t == 0:
                            pe.wait_ge(S[kb_free[it.u][0]], kb_free[it.u][1])
                        for a in range(4):
                            for j in range(2):
                                m = pe.matmul(zS[:, st.z.s, 0, a * NCMP:(a + 1) * NCMP], qT[:, a, it.t * P:(it.t + 1) * P], kbT[:, j, :],
                                              start=j == 0, stop=j == 1)
                        hit(m, "pe_z")
                    elif kd == "S":
                        it = st.it
                        a, t = it.lanes[st.a]
                        wait(pe, st.z.before)
                        wait(pe, tr_free[it.u])
                        x = {"slc": 0, "win": 1}.get(it.br, a)
                        c0, c1 = it.k0 * P, (t + 1) * P
                        out = zS[:, st.z.s].rearrange("p b n -> p (b n)")
                        for g0 in range(c0, c1, 512):
                            g1 = min(g0 + 512, c1)
                            o = out[:, g0 - c0:g1 - c0]
                            q = qT[:, a, t * P:(t + 1) * P]
                            pe.matmul(o, q, kT[:, 2 * x, g0:g1], start=True, stop=False)
                            if g1 == c1:
                                pe.matmul(o[:, g1 - P - g0:g1 - g0], ident_b[:], late_b[:], start=False, stop=False)
                            if it.br == "win" and t >= WT and g0 == c0:
                                pe.matmul(o[:, 0:P], ident_b[:], early_b[:], start=False, stop=False)
                            m = pe.matmul(o, q, kT[:, 2 * x + 1, g0:g1], start=False, stop=True)
                        hit(m, "pe_z")
                    elif kd == "T":
                        it = st.it
                        wait(pe, it.p_done)
                        wait(pe, st.t.before)
                        for a in st.lanes:
                            if it.br == "cmp":
                                m = pe.transpose(tS[0:NCMP, st.t.s, a * P:(a + 1) * P], cmp_pr[:, it.i // 3 % 2, a, :], ident[:])
                            else:
                                j = (st.kb - it.k0) * P
                                m = pe.transpose(tS[:, st.t.s, a * P:(a + 1) * P], prob[:, it.buf, a, j:j + P], ident[:])
                        hit(m, "pe_t")
                    elif kd == "PV":
                        it = st.it
                        if st.first:
                            wait(pe, it.o.before)
                        wait(pe, st.t.free)
                        x = {"slc": 0, "win": 1, "cmp": 0}.get(it.br, it.get("h", 0))
                        n = NCMP if it.br == "cmp" else P
                        lhs = vb[:, :] if it.br == "cmp" else V[:, st.kb, x, :]
                        c0 = st.lanes[0] * P
                        for j, pt in enumerate((pt_hi, pt_lo)):
                            m = pe.matmul(oS[:, it.o.s, c0:512], lhs, pt[0:n, st.pt % 2, c0:512], start=st.first and j == 0, stop=st.last and j == 1)
                        hit(m, "pv_done")
                    elif kd == "OT":
                        it = st.it
                        wait(pe, it.o.free)
                        wait(pe, st.t.before)
                        for a in range(4):
                            m = pe.transpose(tS[:, st.t.s, a * P:(a + 1) * P], oT[:, a * P:(a + 1) * P], ident[:])
                        hit(m, "pe_t")
                    elif kd == "s_begin":
                        pe.wait_ge(S["s_begin"], 1)
                        pe.wait_ge(S["s_rows_in"], 16)
                    elif kd == "s_rep":
                        wait(pe, st.z.before)
                        hit(pe.matmul(zS[:, st.z.s, 0, 0:st.width], SC["seq_T"][0:NB, :], SRt[:, st.c:st.c + st.width], start=True, stop=True), "pe_z")
                    elif kd == "s_decay":
                        pe.wait_ge(S["s_dve"], st.tot)
                        wait(pe, st.t.before)
                        pe.matmul(tS[:, st.t.s, 0:HB], SC["suffix"], cl[:, 63, :], start=True, stop=True)
                        hit(pe.matmul(tS[:, st.t.s, 8:8 + HB], SC["seq_T"][0:NB, :], lf[0:NB, 0, T, :], start=True, stop=True), "pe_t")
                    elif kd == "s_soft":
                        H = HB if st.br.startswith("fox") else HA
                        pe.wait_ge(S["s_dve"], st.nm)
                        wait(pe, st.t1.before)
                        hit(pe.transpose(tS[0:H, st.t1.s, 0:P], SM["nm"][:, 0:H], ident[:]), "pe_t")
                        pe.wait_ge(S["s_dve"], st.nx)
                        wait(pe, st.t2.before)
                        hit(pe.transpose(tS[:, st.t2.s, 0:H], nmx[0:H].rearrange("p b j -> p (b j)"), ident[0:H, 0:H]), "pe_t")
                        pe.wait_ge(S["s_dve"], st.dn)
                        wait(pe, st.t3.before)
                        hit(pe.matmul(tS[:, st.t3.s, 0:H], SC["same"], SM["dn"][:, 0:H], start=True, stop=True), "pe_t")
                    elif kd == "s_select":
                        pe.wait_ge(S["s_dve"], st.a)
                        wait(pe, st.t1.before)
                        hit(pe.matmul(tS[0:NB, st.t1.s, 0:32], SC["seq"], pr[:, 0:32], start=True, stop=True), "pe_t")
                        pe.wait_ge(S["s_dve"], st.b)
                        wait(pe, st.t2.before)
                        hit(pe.matmul(tS[:, st.t2.s, 0:32], SC["seq_T"][0:NB, :], SM["ns"][0:NB].rearrange("p a b -> p (a b)"),
                                      start=True, stop=True), "pe_t")
                    elif kd == "s_v":
                        fox = st.br.startswith("fox")
                        H, w = (HB, 256) if fox else (HA, P)
                        pe.wait_ge(S["px_ready"], st.px)
                        if st.first:
                            wait(pe, st.o.before)
                        if st.br == "cmp":
                            v = kbm[:]
                        elif st.new:
                            v = NF[:].unsqueeze(1) if fox else NK[:, {"slc": 0, "win": 1}[st.br], :].unsqueeze(1)
                        else:
                            v = kv[:, st.n % 4, :].rearrange("p (t c) -> p t c", c=2 * w)
                        for j in range(st.tok):
                            q = pw[:, j * NB * H:(j + 1) * NB * H]
                            m = pe.matmul(oS[0:NB * H, st.o.s, 0:w], q, v[:, j, w:2 * w], start=st.first and j == 0,
                                          stop=st.last and j == st.tok - 1)
                        hit(m, "sv_done")
                    elif kd == "s_o":
                        fox = st.br.startswith("fox")
                        if fox:
                            for ca, t in zip(st.ca, st.ta):
                                pe.wait_ge(S["s_dve"], ca)
                                wait(pe, t.before)
                                hit(pe.matmul(tS[0:32, t.s, 0:1], pw[:, 0:32], SC["inv16"], start=True, stop=True), "pe_t")
                        pe.wait_ge(S["s_dve"], st.spread)
                        wait(pe, st.z.before)
                        n, w, sel = (32, 256, SC["frow_seq"]) if fox else (64, 512, SC["row_seq"])
                        hit(pe.matmul(zS[0:NB, st.z.s, 0, 0:w], sel[0:n, :], wrow[0:n, 0:w], start=True, stop=True), "pe_z")
                    elif kd == "s_ret":
                        pe.wait_ge(S["s_dve"], st.part)
                        wait(pe, st.z.before)
                        hit(pe.matmul(zS[0:NB, st.z.s, 0, 0:256], SC["seq"], pr[:, 0:256], start=True, stop=True), "pe_z")
                        pe.wait_ge(S["s_dve"], st.end)
                pe.sem_inc(S["ends"], 1)
                pe.wait_ge(S["next_layer"], l + 1)

        @block.scalar
        def _(act):
            A = act.activation

            def done(ins, name="act_step", value=None):
                n = hit(ins, name)
                act.wait_ge(S[name], value or n)

            act.wait_ge(S["start"], 2)
            with act.Fori(0, DEPTH) as l:
                for st in steps:
                    kd = st.kind
                    if kd == "x":
                        r = st.r
                        act.wait_ge(S[f"x_in{r % 2}"], 16 * (r // 2 + 1))
                        if r >= 2:
                            act.wait_ge(S["x_rs"], r - 1)
                        n = rows(r)
                        done(A(x_sq[0:n, :], x_t[0:n, r % 2, :], ACT.Square, accum_out=TN["xss"][0:n, r % 2:r % 2 + 1]), "x_sq")
                    elif kd in ("xt", "mt"):
                        r = st.r
                        if kd == "mt":
                            act.wait_ge(S["pe_z"], st.wait_z)
                        for i, t in enumerate(st.t):
                            act.wait_ge(S["pe_t"], t.up)
                            if r == T:
                                out, n = xs_hi[:], NB
                            else:
                                out = (big_hi[:, 4 * i:4 * i + 4, r * P:(r + 1) * P] if kd == "xt" else mt_hi[:, r % 2, 4 * i:4 * i + 4, :])
                                n = P
                            w = out.shape[1] * n
                            done(A(out, tS[:, t.s, 0:w].rearrange("p (k n) -> p k n", n=n), ACT.Copy), "split_hi")
                    elif kd == "w":
                        n = st.n
                        act.wait_ge(S[f"w_in{n % 3}"], 16 * (n // 3 + 1))
                        if st.k == 0:
                            if st.wait_z:
                                act.wait_ge(S["pe_z"], st.wait_z)
                            if st.wait_f:
                                act.wait_ge(S["att_done"], st.wait_f)
                        if st.u < len(UNITS):
                            w = UNITS[st.u]["width"]
                            done(A(w_hi[:, st.k, 0:w], raw[:, n % 3, 0:w], ACT.Copy), "w_hi")
                        else:
                            done(A(big_hi[:, st.k, :], raw[:, n % 3, :], ACT.Copy), "w_hi")
                    elif kd == "z":
                        r, z, unit = st.r, st.z, UNITS[st.u]
                        n = rows(r)
                        act.wait_ge(S["pe_z"], z.up)
                        if unit["kind"] == "gate":
                            done(A(ge[0:n, z.n % 2, :], zS[0:n, z.s, 0, :], ACT.Exp, scale=-1.0), "gate_e")
                            continue
                        b = st.b
                        if st.tiles >= 2:
                            act.wait_ge(S["y_ready"], st.tiles - 1)
                        if st.wait_t:
                            act.wait_ge(S["pe_t"], st.wait_t)
                        if st.y_out:
                            act.wait_ge(S[f"y_out{b}"], st.y_out)
                        if unit["kind"] == "nsa":
                            if st.u == 0:
                                done(A(small[0:n, r, :], zS[0:n, z.s, 0, 320:320 + SMALL], ACT.Copy))
                            done(A(Y[0:n, b, :].rearrange("p (s c) -> p s c", s=2), zS[0:n, z.s, :, 0:320], ACT.Copy), *z.free)
                            w = 448
                        else:
                            done(A(Y[0:n, b, 0:384], zS[0:n, z.s, 0, 0:384], ACT.Copy), *z.free)
                            w = 256
                        if unit["kind"] != "ret":
                            if st.ss >= 2:
                                act.wait_ge(S["ss"], st.ss - 1)
                            done(A(sq[0:n, 0:w], Y[0:n, b, 0:w], ACT.Square), "y_in")
                    elif kd == "tr":
                        r = st.r
                        cs = slice(r * P, (r + 1) * P)
                        kind = UNITS[st.u]["kind"]
                        act.wait_ge(S["pe_t"], st.t[0].up)
                        p4 = lambda s, n: tS[:, s, 0:n * P].rearrange("p (a n) -> p a n", n=P)
                        if kind == "ret":
                            s = st.t[0].s
                            done(A(rq_z[0:64, 0, :], tS[0:64, s, 0:P], ACT.Copy))
                            done(A(rq_z[64:128, 1, :], tS[64:128, s, 0:P], ACT.Copy))
                            done(A(rqx_T[:], tS[:, s, P:2 * P], ACT.Copy))
                            done(A(rk_T[:], tS[:, s, 2 * P:3 * P], ACT.Copy), *st.t[0].free)
                        else:
                            m = 4 if kind == "nsa" else 2
                            done(A(qT[:, 0:m, cs], p4(st.t[0].s, m), ACT.Copy), *st.t[0].free)
                            act.wait_ge(S["pe_t"], st.t[1].up)
                            done(A(kT[:, :, cs], p4(st.t[1].s, 4), ACT.Copy), *st.t[1].free)
                    elif kd == "kb":
                        act.wait_ge(S["pe_t"], st.pe)
                        done(A(kvm[:], oS[0:NCMP, st.mean.s, 0:P], ACT.Copy), *st.mean.free)
                        if st.ag:
                            done(A(ag[:], small[:, :, 0:3 * HA], ACT.Exp, scale=-1.0), "ag_exp")
                        act.wait_ge(S["pe_t"], st.t.up)
                        done(A(kbT[:], tS[:, st.t.s, 0:2 * NCMP].rearrange("p (a n) -> p a n", n=NCMP), ACT.Copy), *st.t.free)
                    elif kd == "logf":
                        act.wait_ge(S["lf_abs"], st.a)
                        done(A(lf[:, 1], lf[:, 1], ACT.Exp))
                        done(A(lf[:, 1], lf[:, 1], ACT.Ln, bias=TN["one"]), "lf_ln")
                        for i, t in enumerate(st.t):
                            act.wait_ge(S["pe_t"], t.up)
                            done(A(lfT[:, i * 512:(i + 1) * 512], tS[0:HB, t.s, :], ACT.Copy), *t.free)
                    elif kd == "ro":
                        act.wait_ge(S["pe_o"], st.up)
                        if st.gn:
                            act.wait_ge(S["gn_out"], st.gn)
                        done(A(ro[:, st.r % 2, :], oS[:, st.o.s, 0:P], ACT.Copy), "ret_copy")
                    elif kd == "SC":
                        act.wait_ge(S["cmp_in"], st.cs)
                        done(A(cmp_s0[:], cmp_s0[:], ACT.Exp, scale=-1.0), "cmp_exp")
                    elif kd == "S":
                        it = st.it
                        a, t = it.lanes[st.a]
                        n = (t + 1 - it.k0) * P
                        slot = (st.p - 1) % 8
                        if it.t_before and st.a == 0:
                            act.wait_ge(S["pe_t"], it.t_before)
                        if it.ot_before and st.a == 0:
                            act.wait_ge(S["att_done"], it.ot_before)
                        kw = dict(bias=TN["nm"][:, slot:slot + 1], scale=-1.0, accum_out=TN["den"][:, it.den, st.a:st.a + 1])
                        if st.masked:
                            wait(act, st.z.free)
                            done(A(prob[:, it.buf, st.a, 0:n], prob[:, it.buf, st.a, 0:n], ACT.Exp, **kw), "p_ready")
                        else:
                            act.wait_ge(S["nm_ready"], st.nm)
                            done(A(prob[:, it.buf, st.a, 0:n], zS[:, st.z.s].rearrange("p b n -> p (b n)")[:, 0:n], ACT.Exp, **kw), "p_ready")
                    elif kd == "T":
                        it = st.it
                        n = NCMP if it.br == "cmp" else P
                        act.wait_ge(S["pe_t"], st.t.up)
                        if st.hi > 2:
                            act.wait_ge(S["pv_done"], st.hi - 2)
                        c0 = st.lanes[0] * P
                        done(A(pt_hi[0:n, st.hi % 2, c0:512], tS[0:n, st.t.s, c0:512], ACT.Copy), "pt_hi")
                    elif kd == "OE":
                        it = st.it
                        act.wait_ge(S["pv_done"], st.pv)
                        if st.ot:
                            act.wait_ge(S["pe_t"], st.ot)
                        done(A(oT[:], oS[:, it.o.s, :], ACT.Copy), *it.o.free)
                    elif kd == "s_begin":
                        act.wait_ge(S["s_begin"], 1)
                    elif kd == "s_rep":
                        dst = {"q": QR[:], "new": NK[:].rearrange("p a c -> p (a c)"), "fq": FQ[:], "newf": NF[:],
                               "ret": RR[:].rearrange("p a c -> p (a c)")}[st.dst][:, st.off:st.off + st.width]
                        act.wait_ge(S["pe_z"], st.z.up)
                        done(A(dst, zS[:, st.z.s, 0, 0:st.width], ACT.Copy), *st.z.free)
                    elif kd == "s_soft":
                        H = HB if st.br.startswith("fox") else HA
                        act.wait_ge(S["s_dve"], st.e_in)
                        done(A(ssc_of(st), ssc_of(st), ACT.Exp, scale=-1.0), "s_act")
                    elif kd == "s_keep":
                        act.wait_ge(S["sv_done"], sv_before[id(st)])
                        done(A(OA[:], oS[0:32, st.o.s, 0:256], ACT.Copy), *st.o.free)
                    elif kd == "s_o":
                        fox = st.br.startswith("fox")
                        n, w = (32, 256) if fox else (64, P)
                        act.wait_ge(S["sv_done"], sv_before[id(st)])
                        if prev_so[id(st)]:
                            act.wait_ge(S["s_dve"], prev_so[id(st)])
                        done(A(orow[0:n, 0:w], oS[0:n, st.o.s, 0:w], ACT.Copy), *st.o.free)
                        if fox:
                            act.wait_ge(S["s_fox"], 1)
                            done(A(SM["fa"], SM["fa"], ACT.Exp, scale=-1.0), "s_foxe")
                            done(A(SM["fb"], SM["fb"], ACT.Exp, scale=-1.0), "s_foxe")
                    elif kd == "s_ret":
                        act.wait_ge(S["s_dve"], st.end)
                        act.wait_ge(S["s_end"], 1)
                act.sem_inc(S["ends"], 1)
                act.wait_ge(S["next_layer"], l + 1)

        @block.vector
        def _(dve):
            TT, TS, STT, CP = dve.tensor_tensor, dve.tensor_scalar, dve.scalar_tensor_tensor, dve.tensor_copy

            def done(ins, name="dve_step", value=None):
                n = hit(ins, name)
                dve.wait_ge(S[name], value or n)

            def indices(name):
                done(TT(idx_f[:], base_f[:].to_broadcast([P, 13]), SC["idx_mul"], ALU.mult), name)
                done(TT(idx_f[:], idx_f[:], SC["idx_add"], ALU.add), name)
                done(CP(idx_u[:, :, 0], idx_f[:]), name)

            def rope(x, tmp, cos, sin, n):
                H = x.shape[1]
                h2 = HD // 2
                done(TT(tmp[:, :, 0:h2], x[:, :, h2:HD], bc(sin[:, 0:h2], 1, H), ALU.mult))
                done(TT(tmp[:, :, h2:HD], x[:, :, 0:h2], bc(sin[:, h2:HD], 1, H), ALU.mult))
                done(TT(x, x, bc(cos, 1, H), ALU.mult))
                done(TT(x, x, tmp, ALU.add))

            def reduce(out, in_, op=ALU.add, name="dve_step", value=None):
                done(dve.tensor_reduce(out=out, in_=in_, op=op, axis=AX.X), name, value)

            done(dve.memset(TN["one"], 1.0), "pro_dve")
            done(dve.memset(TN["halfneg"], -0.5), "pro_dve")
            done(dve.memset(small[:, T, :], 0.0), "pro_dve")
            dve.wait_ge(S["consts_in"], 48)
            dve.wait_ge(S["pages_in"], 48)
            done(TS(base_f[:], pages[:], 2.0, None, ALU.mult), "pro_dve")
            done(TT(base_f[:], base_f[:], SC["half"], ALU.add), "pro_dve")
            indices("pro_dve")
            dve.sem_inc(S["start"], 1)
            dve.wait_ge(S["start"], 2)

            with dve.Fori(0, DEPTH) as l:
                stored = {0: 0, 1: 0}
                mixed = {0: 0, 1: 0}
                gn_n = 0
                ret_stores = 0
                px_before = 0
                for st in steps:
                    kd = st.kind
                    if kd == "x":
                        r, n, b = st.r, rows(st.r), st.r % 2
                        if r == 0:
                            dve.wait_ge(S["norm_in"], 16)
                        dve.wait_ge(S["x_rs"], r + 1)
                        if st.pe:
                            dve.wait_ge(S["pe_t"], st.pe)
                        done(STT(xn[0:n, b, :], x_t[0:n, b, :], TN["xrs"][0:n, b:b + 1], norm_row[0:n, :], ALU.mult, ALU.mult), "xn_ready")
                    elif kd in ("xt", "mt"):
                        r = st.r
                        for i, t in enumerate(st.t):
                            dve.wait_ge(S["split_hi"], st.hi[i])
                            if r == T:
                                hi, lo, n = xs_hi[:], xs_lo[:], NB
                            elif kd == "xt":
                                hi, lo = (x[:, 4 * i:4 * i + 4, r * P:(r + 1) * P] for x in (big_hi, big_lo))
                                n = P
                            else:
                                hi, lo = (x[:, r % 2, 4 * i:4 * i + 4, :] for x in (mt_hi, mt_lo))
                                n = P
                            w = hi.shape[1] * n
                            done(TT(lo, tS[:, t.s, 0:w].rearrange("p (k n) -> p k n", n=n), hi.bitcast(F32), ALU.subtract), *t.free)
                    elif kd == "w":
                        n, k = st.n, st.k
                        dve.wait_ge(S["w_hi"], n + 1)
                        if st.u < len(UNITS):
                            w = UNITS[st.u]["width"]
                            done(TT(w_lo[:, k, 0:w], raw[:, n % 3, 0:w], w_hi[:, k, 0:w].bitcast(F32), ALU.subtract), "w_split")
                        else:
                            done(TT(big_lo[:, k, :], raw[:, n % 3, :], big_hi[:, k, :].bitcast(F32), ALU.subtract), "w_split")
                    elif kd == "z":
                        r, z, unit = st.r, st.z, UNITS[st.u]
                        n = rows(r)
                        if unit["kind"] in ("nsa", "fox"):
                            H = 7 if unit["kind"] == "nsa" else 4
                            dve.wait_ge(S["y_in"], st.ysq)
                            if st.rs > 2:
                                dve.wait_ge(S["rs"], st.rs - 2)
                            reduce(TN["ss"][0:n, st.ss % 2, 0:H], heads(sq[0:n, 0:H * HD]), name="ss")
                        elif unit["kind"] == "gate":
                            half, b = unit["i"], z.n % 2
                            cs = slice(half * 512, (half + 1) * 512)
                            dve.wait_ge(S["gate_e"], st.e)
                            done(TS(ge[0:n, b, :], ge[0:n, b, :], 1.0, None, ALU.add))
                            done(dve.reciprocal(ge[0:n, b, :], ge[0:n, b, :]))
                            if r < T:
                                g = half * T + r
                                dve.wait_ge(S[f"mix_in{g % 2}"], 16 * (g // 2 + 1))
                                done(TT(ge[:, b, :], ge[:, b, :], mixl[:, g % 2, :], ALU.mult))
                                done(TT(gated[:, r, cs], ge[:, b, :], zS[:, z.s, 0, :], ALU.mult), *z.free)
                            else:
                                done(TT(ge[0:n, b, :], ge[0:n, b, :], mixs[:, cs], ALU.mult))
                                done(TT(gated_s[:, cs], ge[0:n, b, :], zS[0:n, z.s, 0, :], ALU.mult), *z.free)
                    elif kd == "y":
                        r, z, unit = st.r, st.z, UNITS[st.u]
                        n, b, kind, i = rows(r), z.b, unit["kind"], unit["i"]
                        cos, sin = (C["rope"][:, r, 0, :], C["rope"][:, r, 1, :]) if r < T else (rope_s[0:n, 0, :], rope_s[0:n, 1, :])
                        if st.u == 0 and r == 0:
                            dve.wait_ge(S["row_w_in"], 64)
                        H = 7 if kind == "nsa" else 4
                        x = heads(Y[0:n, b, 0:H * HD])
                        rt = heads(rot[0:n, 0:H * HD])
                        slots = heads(Y[0:n, b, :])
                        if kind == "ret":
                            wait(dve, z.z.free)
                            if r == 0:
                                if ret_stores:
                                    dve.wait_ge(S["ret_st"], 16 * ret_stores)
                                done(dve.memset(rstate[:], 0.0))
                                done(dve.memset(rq_z[:], 0.0))
                                done(dve.memset(rvz[:], 0.0))
                            rope(x, rt, cos, sin, n)
                            done(TS(Y[0:n, b, 128:256], Y[0:n, b, 128:256], float(SCALE), None, ALU.mult), *(("y_ready",) if r == T else ()))
                        else:
                            dve.wait_ge(S["rs"], z.rs)
                            if (kind, i, r) == ("fox", 0, 0):
                                dve.wait_ge(S["c_out"], 16)
                            done(TT(x, x, TN["rs"][0:n, z.rs % 2, 0:H].unsqueeze(2).to_broadcast([n, H, HD]), ALU.mult))
                            wt = w7 if kind == "nsa" else w4
                            done(TT(Y[0:n, b, 0:H * HD], Y[0:n, b, 0:H * HD], wt[0:n, :], ALU.mult))
                            if kind == "nsa":
                                rope(x, rt, cos, sin, n)
                        if r == T:
                            stored[b] += 16 * y_stores(unit, r)
                            if kind != "ret":
                                w = 256 if kind == "nsa" else P
                                done(TS(Y[0:n, b, 0:w], Y[0:n, b, 0:w], -float(SCALE), None, ALU.mult), "y_ready")
                            continue
                        dve.wait_ge(S["pe_t"], st.wait_t)
                        if kind == "ret":
                            if st.wait_o:
                                dve.wait_ge(S["pe_o"], st.wait_o)
                            stored_v = slots[:, 4:6, :]
                            done(CP(rk[:, b, :], Y[:, b, 128:256]))
                            done(TT(heads(rqx[:, b, :]), slots[:, 0:2, :], C["xi"][:, 2 * i:2 * i + 2].unsqueeze(2).to_broadcast([P, 2, HD]), ALU.mult))
                            for h in range(2):
                                done(CP(rvz[:, b, h, h * HD:(h + 1) * HD], stored_v[:, h, :]))
                            done(TT(heads(rzv[:, b, :]), stored_v, C["zeta"][:, 2 * i:2 * i + 2].unsqueeze(2).to_broadcast([P, 2, HD]), ALU.mult), "y_ready")
                            continue
                        m = 4 if kind == "nsa" else 2
                        sp = split[:, b, :]
                        q2 = sp[:, 0:2 * m * HD].rearrange("p (m t d) -> p m t d", t=2, d=HD)
                        qs = slots[:, 0:m, :]
                        done(TS(q2[:, :, 0, :].bitcast(F32R), qs, -float(SCALE), None, ALU.mult))
                        done(STT(q2[:, :, 1, :], qs, -float(SCALE), q2[:, :, 0, :], ALU.mult, ALU.subtract))
                        k4 = sp[:, 512:1024].rearrange("p (m t d) -> p m t d", t=4, d=HD)
                        ks = slots[:, 4:6, :] if kind == "nsa" else slots[:, 2:4, :]
                        ks2 = bc(ks, 2, 2)
                        done(CP(k4[:, :, 0:2, :].bitcast(F32R), ks2))
                        done(TT(k4[:, :, 2:4, :], ks2, k4[:, :, 0:2, :], ALU.subtract))
                        vs = slots[:, 8:10, :] if kind == "nsa" else slots[:, 4:6, :]
                        done(CP(V[:, r, :, 0:HD], vs))
                        done(TT(V[:, r, :, HD:P], vs, V[:, r, :, 0:HD].bitcast(F32), ALU.subtract), "y_ready")
                        stored[b] += 16 * y_stores(unit, r)
                    elif kd == "kb":
                        wait(dve, st.mean.free)
                        k4 = kbr[:].rearrange("p (t d) -> p t d", d=HD)
                        ks = bc(kvm[:, 0:HD], 1, 2)
                        done(CP(k4[:, 0:2, :].bitcast(F32R), ks))
                        done(TT(k4[:, 2:4, :], ks, k4[:, 0:2, :], ALU.subtract))
                        done(CP(vb[:, 0:HD], kvm[:, HD:P]))
                        done(TT(vb[:, HD:P], kvm[:, HD:P], vb[:, 0:HD].bitcast(F32), ALU.subtract), "kb_split")
                        if st.ag:
                            dve.wait_ge(S["ag_exp"], st.ag)
                            done(TS(ag[:], ag[:], 1.0, None, ALU.add))
                            done(dve.reciprocal(ag[:], ag[:]))
                    elif kd == "logf":
                        done(TT(lf[:, 0], small[:, :, 3 * HA:SMALL], bc(bf_row[:], 1, T + 1), ALU.add))
                        done(TS(lf[:, 1], lf[:, 0], -1.0, None, ALU.mult))
                        done(TT(lf[:, 1], lf[:, 0], lf[:, 1], ALU.min), "lf_abs")
                        dve.wait_ge(S["lf_ln"], st.b)
                        done(STT(lf[:, 0], lf[:, 0], 0.0, lf[:, 1], ALU.min, ALU.subtract), "lf_ready")
                        wait(dve, st.t[1].free)
                        done(dve.tensor_tensor_scan(cT[:], lfT[:], lfT[:], 0.0, ALU.add, ALU.bypass), "lf_scan")
                    elif kd == "ra":
                        i = UNITS[st.u]["i"]
                        dve.wait_ge(S["pe_o"], st.up)
                        done(TT(rat[:], oS[:, st.o.s, 0:256].rearrange("p (h n) -> p h n", h=2), C["decay"][:, 2 * i:2 * i + 2, :], ALU.mult), *st.o.free)
                    elif kd == "ro":
                        i, b = UNITS[st.u]["i"], st.r % 2
                        dve.wait_ge(S["ret_copy"], st.c)
                        for h in range(2):
                            hs = slice(h * HD, (h + 1) * HD)
                            ins = STT(rstate[hs, hs], rstate[hs, hs], G_CHUNK[2 * i + h], oS[hs, st.o.s, P + h * HD:P + (h + 1) * HD], ALU.mult, ALU.add)
                            if h:
                                done(ins, *st.o.free)
                            else:
                                done(ins)
                        x = heads(ro[:, b, :])
                        if st.rs > 2:
                            dve.wait_ge(S["gn_rs"], st.rs - 2)
                        reduce(TN["mu"][:, b, :], x)
                        done(TS(TN["mu"][:, b, :], TN["mu"][:, b, :], 1.0 / HD, None, ALU.mult))
                        done(TT(x, x, TN["mu"][:, b, :].unsqueeze(2).to_broadcast([P, 2, HD]), ALU.subtract))
                        done(TT(ro_sq[:], ro[:, b, :], ro[:, b, :], ALU.mult))
                        reduce(TN["gss"][:, b, :], heads(ro_sq[:]), name="gn_sq")
                    elif kd == "gn":
                        i, b = UNITS[st.u]["i"], st.r % 2
                        dve.wait_ge(S["gn_rs"], st.rs)
                        x = heads(ro[:, b, :])
                        done(TT(x, x, TN["grs"][:, b, :].unsqueeze(2).to_broadcast([P, 2, HD]), ALU.mult))
                        if gn_n >= 2:
                            dve.wait_ge(S[f"mx_out{b}"], 16 * (gn_n // 2))
                        done(TT(ret_mix[:, b, :], ro[:, b, :], gn_row[:, i * P:(i + 1) * P], ALU.mult), "gn_out")
                        gn_n += 1
                    elif kd == "ret_state":
                        ret_stores += 2
                    elif kd == "SC":
                        it = st.it
                        t = it.t
                        dve.wait_ge(S["pe_z"], st.z.up)
                        if it.i == 0:
                            for b in range(2):
                                dve.wait_ge(S[f"y_out{b}"], stored[b])
                        flat = cmp_s0[:].rearrange("p a n -> p (a n)")
                        done(TT(cmp_s0[:], zS[:, st.z.s, 0, 0:P].rearrange("p (a n) -> p a n", a=4), bc(C["bias"][:, t, :], 1, 4), ALU.add), *st.z.free)
                        reduce(TN["cnm"], cmp_s0[:], ALU.min)
                        done(TT(cmp_s0[:], cmp_s0[:], TN["cnm"].unsqueeze(2).to_broadcast([P, 4, NCMP]), ALU.subtract), "cmp_in")
                        dve.wait_ge(S["cmp_exp"], st.e)
                        done(TT(cmp_s0[:], cmp_s0[:], bc(C["keep"][:, t, :], 1, 4), ALU.mult))
                        reduce(TN["cden"], cmp_s0[:])
                        done(TS(TN["cden"], TN["cden"], 0.5, None, ALU.max))
                        done(dve.reciprocal(TN["cden"], TN["cden"]))
                        if it.c_before:
                            dve.wait_ge(S["pe_t"], it.c_before)
                        cp = cmp_pr[:, it.i // 3 % 2]
                        done(TT(cp, cmp_s0[:], TN["cden"].unsqueeze(2).to_broadcast([P, 4, NCMP]), ALU.mult), "cmp_p")
                        if t >= 4:
                            reduce(imp4[:].rearrange("p a j -> p (a j)"), cp.rearrange("p a (j r) -> p (a j) r", r=2))
                            reduce(TN["imp"][:, 0:NSEL], imp4[:].rearrange("p a j -> p j a"))
                            done(TT(TN["imp"][:, 0:NSEL], TN["imp"][:, 0:NSEL], C["sel_mul"][:, t - 4, :], ALU.mult))
                            done(TT(TN["imp"][:, 0:NSEL], TN["imp"][:, 0:NSEL], C["sel_add"][:, t - 4, :], ALU.add))
                            done(dve.max(TN["m8"], TN["imp"][:, 0:NSEL]))
                            done(dve.match_replace(TN["rep"][:, 0:NSEL], TN["m8"], TN["imp"][:, 0:NSEL], -2.0))
                            done(TS(bm[:, t, :], TN["rep"][:, 0:NSEL], -1.5, BIG, ALU.is_gt, ALU.mult))
                    elif kd == "S":
                        it = st.it
                        a, t = it.lanes[st.a]
                        n = (t + 1 - it.k0) * P
                        slot = (st.p - 1) % 8
                        if st.p > 8:
                            dve.wait_ge(S["p_ready"], st.p - 8)
                        dve.wait_ge(S["pe_z"], st.z.up)
                        zf = zS[:, st.z.s].rearrange("p b n -> p (b n)")[:, 0:n]
                        nm = TN["nm"][:, slot:slot + 1]
                        if st.masked:
                            if it.t_before:
                                dve.wait_ge(S["pe_t"], it.t_before)
                            out = prob[:, it.buf, st.a, 0:n]
                            if it.br == "slc":
                                out, zf = heads(out), heads(zf)
                                add = bm[:, t, 0:n // HD].unsqueeze(2).to_broadcast([P, n // HD, HD])
                            else:
                                if it.h == 0 and it.i == 0 and st.a == 0:
                                    dve.wait_ge(S["c_in"], 16 * (UNITS[it.u]["i"] + 1))
                                add = crow[:, it.h, 0:n]
                            done(dve.tensor_tensor_reduce(out=out, in0=zf, in1=add, scale=1.0, scalar=3e38, op0=ALU.add, op1=ALU.min,
                                                          accum_out=nm), *st.z.free)
                        else:
                            reduce(nm, zf, ALU.min, "nm_ready")
                    elif kd == "T":
                        it = st.it
                        n = NCMP if it.br == "cmp" else P
                        dve.wait_ge(S["pt_hi"], st.hi)
                        c0 = st.lanes[0] * P
                        done(TT(pt_lo[0:n, st.hi % 2, c0:512], tS[0:n, st.t.s, c0:512], pt_hi[0:n, st.hi % 2, c0:512].bitcast(F32), ALU.subtract), *st.t.free)
                    elif kd == "OT":
                        it = st.it
                        t, i, br, b = it.t, UNITS[it.u]["i"], it.br, it.acc % 2
                        co = TN["co"]
                        if br == "fox":
                            done(dve.reciprocal(co, TN["den"][:, it.den, :]))
                            if it.i == 0:
                                for j in range(2):
                                    dve.wait_ge(S[f"y_out{j}"], stored[j])
                        else:
                            gate = ag[:, t, 12 * i:12 * i + 12].rearrange("p (a c) -> p a c", c=3)[:, :, {"cmp": 0, "slc": 1, "win": 2}[br]]
                            if br == "cmp":
                                done(CP(co, gate))
                            else:
                                done(dve.reciprocal(co, TN["den"][:, it.den, :]))
                                done(TT(co, co, gate, ALU.mult))
                        dve.wait_ge(S["pe_t"], st.t.up)
                        done(TT(fin[:], tS[:, st.t.s, :].rearrange("p (a d) -> p a d", a=4), co.unsqueeze(2).to_broadcast([P, 4, P]), ALU.mult), *st.t.free)
                        av = heads(acc[:, b, :])
                        if br in ("cmp", "fox"):
                            if it.acc >= 2:
                                dve.wait_ge(S[f"mix_out{b}"], 16 * (it.acc // 2))
                            done(TT(av, fin[:, :, 0:HD], fin[:, :, HD:P], ALU.add), "att_done")
                        else:
                            done(TT(fin[:, :, 0:HD], fin[:, :, 0:HD], fin[:, :, HD:P], ALU.add))
                            done(TT(av, av, fin[:, :, 0:HD], ALU.add), "att_done")
                    elif kd == "out":
                        r, n, z = st.r, rows(st.r), st.z
                        dve.wait_ge(S[f"res_in{r % 2}"], 16 * (r // 2 + 1))
                        dve.wait_ge(S["pe_z"], z.up)
                        done(TT(res[0:n, r % 2, :], zS[0:n, z.s].rearrange("p b n -> p (b n)"), res[0:n, r % 2, :], ALU.add), *z.free)
                    elif kd == "s_begin":
                        dve.wait_ge(S["pe_o"], st.pe_o)
                        dve.wait_ge(S["mx_out0"], 16 * T)
                        dve.wait_ge(S["mx_out1"], 16 * T)
                        dve.wait_ge(S["ret_st"], 16 * ret_stores)
                        for b in range(2):
                            dve.wait_ge(S[f"y_out{b}"], stored[b])
                        done(dve.memset(ssc[:, 64, 0:1], 0.0), "s_begin")
                    elif kd == "s_rep":
                        last_rep = st.z.free
                    elif kd == "s_decay":
                        dve.wait_ge(S["lf_in"], 16 * (l + 1))
                        for h in range(HB):
                            done(dve.tensor_tensor_scan(cl[:, 0:64, h], lf_t[:, :, h], lf_t[:, :, h], 0.0, ALU.add, ALU.bypass),
                                 *(("s_dve", st.tot) if h == HB - 1 else ()))
                        dve.wait_ge(S["pe_t"], st.t.up)
                        done(TT(cl[:, 0:64, :], cl[:, 0:64, :], bc(tS[:, st.t.s, 0:HB], 1, 64), ALU.add))
                        done(TT(cl[:, 64, :], tS[:, st.t.s, 8:8 + HB], SC["newm"].to_broadcast([P, HB]), ALU.add), *st.t.free)
                        for name in last_reps:
                            wait(dve, name)
                    elif kd == "s_mean":
                        dve.wait_ge(S[f"kv_in{st.n % 4}"], l * KV_IN[st.n % 4] + 16 * (st.n // 4 + 1))
                        src = kv[:, st.n % 4, :].rearrange("p (t c) -> p c t", c=256)
                        if st.c % 2 == 0:
                            reduce(kbm[:, st.c // 2, :], src, name="kv_used")
                        else:
                            reduce(pr[:, 0:256], src, name="kv_used")
                            done(TT(kbm[:, st.c // 2, :], kbm[:, st.c // 2, :], pr[:, 0:256], ALU.add))
                            done(TS(kbm[:, st.c // 2, :], kbm[:, st.c // 2, :], 1.0 / L_CMP, None, ALU.mult))
                    elif kd == "s_k":
                        fox = st.br.startswith("fox")
                        tok = st.tok
                        if st.n is not None:
                            dve.wait_ge(S[f"kv_in{st.n % 4}"], l * KV_IN[st.n % 4] + 16 * (st.n // 4 + 1))
                        H = HB if fox else HA
                        if st.br == "cmp":
                            k = kbm[:, :, 0:P]
                        else:
                            k = kv[:, st.n % 4, :].rearrange("p (t c) -> p t c", t=tok)[:, :, 0:256 if fox else P]

                        def score(k, t0, n):
                            out = ssc[:].rearrange("p t h -> p (t h)")[:, t0 * H:(t0 + n) * H].rearrange("p (t h) -> p t h", h=H)
                            if fox:
                                done(TT(pr[:, 0:n * 256].rearrange("p (t c) -> p t c", c=256), k, bc(FQ[:], 1, n), ALU.mult))
                                reduce(out, pr[:, 0:n * 256].rearrange("p (t h d) -> p t h d", h=H, d=HD))
                                return
                            for g in range(KV):
                                q = heads(QR[:, g * 256:(g + 1) * 256])
                                p4 = pr[:, 0:n * 256].rearrange("p (t h d) -> p t h d", h=GQ, d=HD)
                                done(TT(p4, bc(k[:, :, g * HD:(g + 1) * HD], 2, GQ), bc(q, 1, n), ALU.mult))
                                reduce(out[:, :, g * GQ:(g + 1) * GQ], p4)

                        score(k, st.c * tok, tok)
                        if st.br in ("slc", "win", "foxb") and (st.c + 1) * tok in (32, 64) and (st.br != "slc" or st.c == 3):
                            nk = NF[:, 0:256].unsqueeze(1) if fox else NK[:, {"slc": 0, "win": 1}[st.br], 0:P].unsqueeze(1)
                            score(nk, (st.c + 1) * tok, 1)
                    elif kd == "s_soft":
                        fox = st.br.startswith("fox")
                        H = HB if fox else HA
                        sc = ssc_of(st)
                        by_head = sc.rearrange("p t h -> p h t")
                        N = st.toks
                        if fox:
                            t0 = 0 if st.br == "foxa" else 32
                            done(TT(sc, sc, cl[:, t0:t0 + N, :], ALU.add))
                        elif st.br != "cmp":
                            if st.br == "slc":
                                for g in range(KV):
                                    hs = slice(g * GQ, (g + 1) * GQ)
                                    done(TS(sc[:, :, hs], sc[:, :, hs], SM["bms"][:, g:g + 1], None, ALU.add))
                            else:
                                done(TS(sc[:, 0, :], sc[:, 0, :], SC["win0"], None, ALU.add))
                            done(TS(sc[:, N - 1, :], sc[:, N - 1, :], SC["newm"], None, ALU.add))
                        reduce(SM["nm"][:, 0:H], by_head, ALU.min, "s_dve")
                        dve.wait_ge(S["pe_t"], st.t1.up)
                        reduce(SM["nmb"][0:H, :], tS[0:H, st.t1.s, 0:P].rearrange("p (b j) -> p b j", j=16), ALU.min, *st.t1.free)
                        done(CP(nmx[0:H], SM["nmb"][0:H, :].unsqueeze(2).to_broadcast([H, NB, 16])), "s_dve")
                        dve.wait_ge(S["pe_t"], st.t2.up)
                        done(CP(SM["NM"][:, 0:H], tS[:, st.t2.s, 0:H]), *st.t2.free)
                        done(TT(sc, sc, bc(SM["NM"][:, 0:H], 1, N), ALU.subtract), "s_dve")
                        dve.wait_ge(S["s_act"], st.e)
                        reduce(SM["dn"][:, 0:H], by_head, name="s_dve")
                        dve.wait_ge(S["pe_t"], st.t3.up)
                        if st.br == "foxa":
                            done(CP(SM["denA"], tS[:, st.t3.s, 0:H]), *st.t3.free)
                            done(CP(SM["NMA"], SM["NM"][:, 0:H]))
                        else:
                            done(CP(SM["rd"][:, 0:H], tS[:, st.t3.s, 0:H]), *st.t3.free)
                            if not fox:
                                done(dve.reciprocal(SM["rd"], SM["rd"]))
                                done(TT(sc, sc, bc(SM["rd"], 1, N), ALU.mult))
                    elif kd == "s_select":
                        p2 = ssc[:].rearrange("p t h -> p (t h)")[:, 0:16].rearrange("p (a h) -> p a h", h=GQ)
                        reduce(SM["tmp4"][:, 0:4], p2)
                        done(TT(SM["imp"], SM["tmp4"][:, 0:2], SM["tmp4"][:, 2:4], ALU.add))
                        done(TT(pr[:, 0:32].rearrange("p (g j) -> p g j", g=2), SM["imp"].unsqueeze(2).to_broadcast([P, 2, 16]),
                                bc(SC["own"], 1, 2), ALU.mult), "s_dve")
                        dve.wait_ge(S["pe_t"], st.t1.up)
                        s8 = SM["sc"][0:NB]
                        done(CP(s8[:, :, NSEL], bc(SC["forced"][0:NB, NSEL:NSEL + 1], 1, 2)[:, :, 0]))
                        done(TT(s8[:, :, 0:NSEL], tS[0:NB, st.t1.s, 0:32].rearrange("p (g j) -> p g j", g=2), bc(SC["forced"][0:NB, 0:NSEL], 1, 2),
                                ALU.add), *st.t1.free)
                        for g in range(KV):
                            done(dve.max(SM["m8"][0:NB], s8[:, g, :]))
                            done(dve.match_replace(SM["rep"][0:NB], SM["m8"][0:NB], s8[:, g, :], -2.0))
                            ins = TS(SM["ns"][0:NB, g, :], SM["rep"][0:NB, 0:NSEL], -1.5, None, ALU.is_gt)
                            if g:
                                done(ins, "s_dve")
                            else:
                                done(ins)
                        dve.wait_ge(S["pe_t"], st.t2.up)
                        p3 = pr[:, 0:32].rearrange("p (g j) -> p g j", g=2)
                        done(TT(p3, tS[:, st.t2.s, 0:32].rearrange("p (g j) -> p g j", g=2), bc(SC["own"], 1, 2), ALU.mult), *st.t2.free)
                        reduce(SM["bms"], p3)
                        done(TS(SM["bms"], SM["bms"], BIG, None, ALU.mult))
                    elif kd == "s_v":
                        fox = st.br.startswith("fox")
                        H = HB if fox else HA
                        if px_before:
                            dve.wait_ge(S["sv_done"], px_before)
                        px_before = st.up
                        t0 = st.c * (8 if fox else 16)
                        if st.br == "cmp":
                            t0 = 0
                        p = ssc[:].rearrange("p t h -> p (t h)")[:, t0 * H:(t0 + st.tok) * H].rearrange("p (t h) -> p t h", h=H)
                        out = pw[:, 0:st.tok * NB * H].rearrange("p (t b h) -> p t b h", b=NB, h=H)
                        done(TT(out, bc(p, 2, NB), bc(bc(SC["seq"], 1, st.tok), 3, H), ALU.mult), "px_ready")
                    elif kd == "s_o":
                        fox = st.br.startswith("fox")
                        z = st.z
                        if not fox:
                            br = {"cmp": 0, "slc": 1, "win": 2}[st.br]
                            wait(dve, st.o.free)
                            done(TT(wrow[:].rearrange("p (g a d) -> p g a d", g=2, a=4), bc(orow[:, 0:P].rearrange("p (g d) -> p g d", g=2), 2, 4),
                                    SC["head_of"][0:64, :].rearrange("p (g a) -> p g a", g=2).unsqueeze(3).to_broadcast([64, 2, 4, HD]), ALU.mult), "s_dve")
                            dve.wait_ge(S["pe_z"], z.up)
                            gate = ag[0:NB, T, :].rearrange("p (h c) -> p h c", c=3)[:, :, br].unsqueeze(2).to_broadcast([NB, HA, HD])
                            zz = heads(zS[0:NB, z.s, 0, :])
                            if br == 0:
                                done(TT(heads(mixs[:, 0:512]), zz, gate, ALU.mult), *z.free)
                            else:
                                done(TT(heads(pr[0:NB, 0:512]), zz, gate, ALU.mult), *z.free)
                                done(TT(mixs[:, 0:512], mixs[:, 0:512], pr[0:NB, 0:512], ALU.add))
                        else:
                            fa, fb, nf = SM["fa"], SM["fb"], SM["nf"]
                            NMB, denB = SM["NM"][:, 0:4], SM["rd"][:, 0:4]
                            done(TT(nf, SM["NMA"], NMB, ALU.min))
                            done(TT(fa, SM["NMA"], nf, ALU.subtract))
                            done(TT(fb, NMB, nf, ALU.subtract), "s_fox")
                            dve.wait_ge(S["s_foxe"], 2)
                            done(TT(nf, fa, SM["denA"], ALU.mult))
                            done(TT(SM["tmp4"][:, 0:4], fb, denB, ALU.mult))
                            done(TT(nf, nf, SM["tmp4"][:, 0:4], ALU.add))
                            done(dve.reciprocal(nf, nf))
                            done(TT(fa, fa, nf, ALU.mult))
                            done(TT(fb, fb, nf, ALU.mult))
                            for f, co, ca, t in ((fa, "coa", st.ca[0], st.ta[0]), (fb, "cob", st.ca[1], st.ta[1])):
                                dve.wait_ge(S["sv_done"], px_before)
                                done(TT(pw[:, 0:32].rearrange("p (b h) -> p b h", h=HB), bc(f, 1, NB), bc(SC["seq"], 2, HB), ALU.mult), "s_dve")
                                dve.wait_ge(S["pe_t"], t.up)
                                done(CP(SM[co][0:32], tS[0:32, t.s, 0:1]), *t.free)
                            wait(dve, st.o.free)
                            done(TS(OA[:], OA[:], SM["coa"][0:32], None, ALU.mult))
                            done(STT(OA[:], orow[0:32, :], SM["cob"][0:32], OA[:], ALU.mult, ALU.add))
                            done(TT(heads(wrow[0:32, 0:256]), heads(OA[:]), SC["fhead_of"][0:32, :].unsqueeze(2).to_broadcast([32, HB, HD]), ALU.mult), "s_dve")
                            dve.wait_ge(S["pe_z"], z.up)
                            done(CP(mixs[:, 512:768], zS[0:NB, z.s, 0, 0:256]), *z.free)
                    elif kd == "s_ret":
                        dve.wait_ge(S["r_in"], 16)
                        p16 = pr[:, 0:256].rearrange("p (j i) -> p j i", j=16)
                        for src, dst in ((0, "qp"), (1, "kp")):
                            done(TT(p16, RR[:, src, :].rearrange("p (j i) -> p j i", j=16), bc(SC["own"], 2, 16), ALU.mult))
                            reduce(SM[dst], p16.rearrange("p j i -> p i j"))
                        hown = SC["hown"].unsqueeze(2).to_broadcast([P, HC, HD])
                        p4 = heads(pr[:, 0:256])
                        done(TT(p4, heads(RR[:, 2, :]), hown, ALU.mult))
                        reduce(vp[:], p4.rearrange("p h d -> p d h"))
                        done(TT(s_t2[:], bc(vp[:], 1, 16), SM["kp"].unsqueeze(2).to_broadcast([P, 16, HD]), ALU.mult))
                        done(STT(s_R[:], s_R[:], SC["g_ret"], s_t2[:], ALU.mult, ALU.add), "s_state")
                        done(TT(s_t1[:], s_R[:], SM["qp"].unsqueeze(2).to_broadcast([P, 16, HD]), ALU.mult))
                        reduce(vp[:], s_t1[:].rearrange("p i d -> p d i"))
                        done(TT(p4, bc(vp[:], 1, HC), hown, ALU.mult), "s_dve")
                        dve.wait_ge(S["pe_z"], st.z.up)
                        o4 = heads(mixs[:, 768:1024])
                        done(CP(mixs[:, 768:1024], zS[0:NB, st.z.s, 0, 0:256]), *st.z.free)
                        mu, ss, rs = (SM[x][0:NB] for x in ("mu", "ss", "rs"))
                        wide = lambda x: x.unsqueeze(2).to_broadcast([NB, HC, HD])
                        reduce(mu, o4)
                        done(TS(mu, mu, 1.0 / HD, None, ALU.mult))
                        done(TT(o4, o4, wide(mu), ALU.subtract))
                        done(TT(pr[0:NB, 0:256], mixs[:, 768:1024], mixs[:, 768:1024], ALU.mult))
                        reduce(ss, heads(pr[0:NB, 0:256]), name="s_dve")
                        dve.wait_ge(S["s_pool"], st.rs)
                        done(TT(o4, o4, wide(rs), ALU.mult))
                        done(TT(mixs[:, 768:1024], mixs[:, 768:1024], gn_row[0:NB, :], ALU.mult), "s_dve")
                        dve.wait_ge(S["s_end"], 1)
                        done(TS(base_f[:], base_f[:], float(2 * N_PHYS), None, ALU.add))
                        indices("dve_step")
                dve.sem_inc(S["ends"], 1)
                dve.wait_ge(S["next_layer"], l + 1)

        @block.gpsimd
        def _(pool):
            def done(ins, name="pool_step", value=None):
                n = hit(ins, name)
                pool.wait_ge(S[name], value or n)

            def rsqrt_mean(out, ss, n, name, value):
                tmp = TN["ptmp"][0:ss.shape[0], 0:ss.shape[1]]
                done(pool.tensor_scalar(tmp, ss, 1.0 / n, EPS, ALU.mult, ALU.add))
                done(pool.tensor_tensor(out, tmp, TN["halfneg"][0:ss.shape[0], 0:ss.shape[1]], ALU.pow), name, value)

            done(pool.memset(ident[:], 0.0), "pro_pool")
            done(pool.affine_select(out=ident[:], in_=ident[:], compare_op=ALU.not_equal, fill=1.0, base=0, pattern=[[-1, P]], channel_multiplier=1), "pro_pool")
            done(pool.memset(ident_b[:], 0.0), "pro_pool")
            done(pool.affine_select(out=ident_b[:], in_=ident_b[:], compare_op=ALU.not_equal, fill=1.0, base=0, pattern=[[-1, P]], channel_multiplier=1), "pro_pool")
            done(pool.memset(late_b[:], 0.0), "pro_pool")
            done(pool.affine_select(out=late_b[:], in_=late_b[:], compare_op=ALU.is_ge, fill=BIG, base=0, pattern=[[-1, P]], channel_multiplier=1), "pro_pool")
            done(pool.memset(early_b[:], 0.0), "pro_pool")
            done(pool.affine_select(out=early_b[:], in_=early_b[:], compare_op=ALU.is_ge, fill=BIG, base=-1, pattern=[[1, P]], channel_multiplier=-1), "pro_pool")
            pool.sem_inc(S["start"], 1)
            pool.wait_ge(S["start"], 2)

            with pool.Fori(0, DEPTH) as l:
                at_layer = lambda t, pat, **k: t[bass.ds(l, 1)].rearrange(pat, **k)

                def gather(n):
                    br, c, tok = CHUNKS[n]
                    w = s_gather_wait(n)
                    if w:
                        wait(pool, w)
                    if br == "win":
                        src = at_layer(state_win, "o b (j c t) k g d -> (o b j) c (t k g d)", j=16, c=2)[:, c, :]
                        hit(pool.dma_start(kv[:, n % 4, :], src), f"kv_in{n % 4}", 16)
                        return
                    cache, col, parts_ = {"cmp": (cache_cmp, c, 4), "slc": (cache_slc, c, 4), "foxa": (cache_fox, 4 + c, 8),
                                          "foxb": (cache_fox, 8 + c, 8)}[br]
                    src = cache.rearrange("l n (h c t) k g d -> (l n h c) (t k g d)", h=2, c=parts_)
                    hit(pool.indirect_dma_start(kv[:, n % 4, :], None, src, bass.IndirectOffsetOnAxis(ap=idx_u[:, col, :], axis=0)),
                        f"kv_in{n % 4}", 16)

                issued = 0
                for st in steps:
                    kd = st.kind
                    if kd == "x":
                        r, n, b = st.r, rows(st.r), st.r % 2
                        pool.wait_ge(S["x_sq"], r + 1)
                        if r >= 2:
                            pool.wait_ge(S["xn_ready"], r - 1)
                        rsqrt_mean(TN["xrs"][0:n, b:b + 1], TN["xss"][0:n, b:b + 1], D, "x_rs", r + 1)
                    elif kd == "z" and UNITS[st.u]["kind"] in ("nsa", "fox"):
                        n, H = rows(st.r), 7 if UNITS[st.u]["kind"] == "nsa" else 4
                        pool.wait_ge(S["ss"], st.ss)
                        if st.rs > 2:
                            pool.wait_ge(S["y_ready"], st.rs - 2)
                        rsqrt_mean(TN["rs"][0:n, st.rs % 2, 0:H], TN["ss"][0:n, st.ss % 2, 0:H], HD, "rs", st.rs)
                    elif kd == "ro":
                        b = st.r % 2
                        pool.wait_ge(S["gn_sq"], st.q)
                        if st.gn:
                            pool.wait_ge(S["gn_out"], st.gn)
                        rsqrt_mean(TN["grs"][:, b, :], TN["gss"][:, b, :], HD, "gn_rs", st.rs)
                    elif kd == "s_begin":
                        pool.wait_ge(S["s_begin"], 1)
                        src = cache_logf.rearrange("l n (h t) g -> (l n h) (t g)", h=2)
                        hit(pool.indirect_dma_start(lf_t[:].rearrange("p t h -> p (t h)"), None, src,
                                                    bass.IndirectOffsetOnAxis(ap=idx_u[:, 12, :], axis=0)), "lf_in", 16)
                        for n in range(len(CHUNKS)):
                            gather(n)
                    elif kd == "s_ret":
                        pool.wait_ge(S["s_dve"], st.q)
                        rsqrt_mean(SM["rs"][0:NB], SM["ss"][0:NB], HD, "s_pool", st.rs)
                pool.sem_inc(S["ends"], 1)
                pool.wait_ge(S["next_layer"], l + 1)

        @block.sync
        def _(sp):
            hit(sp.dma_start(cst[:], consts), "consts_in", 16)
            hit(sp.dma_start(scst[:], s_consts), "consts_in", 16)
            hit(sp.dma_start(rope_s[:].rearrange("p a d -> p (a d)"), rope_new.rearrange("o a d -> o (a d)").to_broadcast([P, 2 * HD])), "consts_in", 16)
            with nc.allow_non_contiguous_dma(reason="64 page ids"):
                for h in range(2):
                    hit(sp.dma_start(pages_d[:, h:h + 1], page_table.rearrange("b (g o) -> (b g) o", o=1)), "pages_in", 16)
            sp.wait_ge(S["pages_in"], 32)
            hit(sp.dma_start(pages[:], pages_d.rearrange("j (h o) -> (j h) o", o=1)), "pages_in", 16)
            hit(sp.dma_start(y_prompt, x_prompt), "copied", 16)
            hit(sp.dma_start(y_sample, x_sample), "copied", 16)
            sp.wait_ge(S["copied"], 32)
            sp.wait_ge(S["consts_in"], 48)
            sp.wait_ge(S["pages_in"], 48)
            sp.wait_ge(S["start"], 2)
            kept = ("kv_in0", "kv_in1", "kv_in2", "kv_in3", "lf_in")
            once = ("start", "pro_dve", "pro_pool", "consts_in", "pages_in", "copied", "ends", "next_layer")

            with sp.Fori(0, DEPTH) as l:
                row = lambda t, w: t[bass.ds(l, 1), :].to_broadcast([P, w])
                hit(sp.dma_start(norm_row[:], row(norm_w, D)), "norm_in", 16)
                hit(sp.dma_start(w7[:], row(w7_in, 7 * HD)), "row_w_in", 16)
                hit(sp.dma_start(w4[:], row(w4_in, 4 * HD)), "row_w_in", 16)
                hit(sp.dma_start(gn_row[:], row(gn_w, HC * HD)), "row_w_in", 16)
                hit(sp.dma_start(bf_row[:], row(fox_bf, HB)), "row_w_in", 16)
                at_layer = lambda t, pat, **k: t[bass.ds(l, 1)].rearrange(pat, **k)
                gate_tiles = []
                for st in sp_steps:
                    kd = st.kind
                    if kd == "x":
                        r, b = st.r, st.r % 2
                        if r >= 2:
                            sp.wait_ge(S["xn_ready"], r - 1)
                        src = y_prompt[0, r * P:(r + 1) * P, :] if r < T else y_sample[:, 0, :]
                        hit(sp.dma_start(x_t[0:rows(r), b, :], src), f"x_in{b}", 16)
                    elif kd == "w":
                        n, k = st.n, st.k
                        if n >= 3:
                            sp.wait_ge(S["w_split"], n - 2)
                        if st.u < len(UNITS):
                            unit = UNITS[st.u]
                            c = unit["off"] * K + k * unit["width"]
                            src = w_in[bass.ds(l, 1), :, c:c + unit["width"]].rearrange("o p n -> (o p) n")
                            hit(sp.dma_start(raw[:, n % 3, 0:unit["width"]], src), f"w_in{n % 3}", 16)
                        else:
                            src = w_out[bass.ds(l, 1), :, k, :].rearrange("o p n -> (o p) n")
                            hit(sp.dma_start(raw[:, n % 3, :], src), f"w_in{n % 3}", 16)
                    elif kd == "crow":
                        sp.wait_ge(S["c_out"], 16)
                        sp.wait_ge(S["att_done"], st.wait_f)
                        src = c_d[2 * st.i:2 * st.i + 2, :].rearrange("(o h) s -> o (h s)", o=1).to_broadcast([P, 2 * SEQ])
                        hit(sp.dma_start(crow[:].rearrange("p h s -> p (h s)"), src), "c_in", 16)
                    elif kd == "s_begin":
                        sp.wait_ge(S["s_begin"], 1)
                        hit(sp.dma_start(SRt[:], s_rows_d), "s_rows_in", 16)
                        for name, t_ in (("cmp", cmp_s), ("slc", slc_s), ("fkv", fox_s)):
                            c, w = SR[name]
                            hit(sp.dma_start(at_layer(t_, "o b t k g d -> (o b) (t k g d)"), s_rows_d[:, c:c + w]), "s_store", 16)
                        c, w = SR["win"]
                        hit(sp.dma_start(win_s[bass.ds(l, 1), :, WINDOW - 1].rearrange("o b k g d -> (o b) (k g d)"), s_rows_d[:, c:c + w]), "s_store", 16)
                        hit(sp.dma_start(at_layer(win_s, "o b t k g d -> (o b) t (k g d)")[:, 0:WINDOW - 1],
                                           at_layer(state_win, "o b t k g d -> (o b) t (k g d)")[:, 1:WINDOW]), "win_shift", 16)
                    elif kd == "s_ret":
                        last_v = [s.up for s in steps if s.kind == "s_v"][-1]
                        sp.wait_ge(S["sv_done"], last_v)
                        hit(sp.dma_start(s_R[:], state_ret[bass.ds(l, 1)].rearrange("o b h (g i) e -> (o b h g) i e", g=4)), "r_in", 16)
                        sp.wait_ge(S["s_state"], 1)
                        hit(sp.dma_start(ret_s[bass.ds(l, 1)].rearrange("o b h (g i) e -> (o b h g) i e", g=4), s_R[:]), "s_store", 16)
                        for i in range(4):
                            sp.wait_ge(S[f"kv_in{i}"], l * KV_IN[i] + KV_IN[i])
                        sp.wait_ge(S["s_store"], fired["s_store"])
                        sp.wait_ge(S["s_dve"], st.end)
                        sp.sem_inc(S["s_end"], 1)
                    elif kd == "z" and UNITS[st.u]["kind"] == "gate" and st.r < T:
                        if st.u == len(UNITS) - 2 and st.r == 0:
                            for name in ("mix_out0", "mix_out1", "mx_out0", "mx_out1"):
                                sp.wait_ge(S[name], fired[name])
                        half, r = UNITS[st.u]["i"], st.r
                        g = half * T + r
                        if g >= 2:
                            wait(sp, gate_tiles[g - 2])
                        gate_tiles.append(st.z.free)
                        hit(sp.dma_start(mixl[:, g % 2, :], mix_d[r * P:(r + 1) * P, half * 512:(half + 1) * 512]), f"mix_in{g % 2}", 16)
                    elif kd == "y" and st.r == T:
                        unit, b = UNITS[st.u], st.z.b
                        i = unit["i"]
                        sp.wait_ge(S["y_ready"], st.up)
                        slots = heads(Y[0:NB, b, :])
                        col = lambda name: s_rows_d[:, SR[name][0]:SR[name][0] + SR[name][1]]
                        if unit["kind"] == "nsa":
                            pairs = [(col("q")[:, i * 256:(i + 1) * 256], Y[0:NB, b, 0:256])]
                            for name, sl in (("cmp", slots[:, 6:8, :]), ("slc", slots[:, 4:9:4, :]), ("win", slots[:, 5:10:4, :])):
                                pairs.append((col(name).rearrange("b (k g d) -> b k g d", g=2, d=HD)[:, :, i, :], sl))
                        elif unit["kind"] == "fox":
                            pairs = [(col("fq")[:, i * P:(i + 1) * P], Y[0:NB, b, 0:P]),
                                     (col("fkv").rearrange("b (k c) -> b k c", k=2)[:, :, i * P:(i + 1) * P],
                                      Y[0:NB, b, P:3 * P].rearrange("p (k c) -> p k c", k=2))]
                        else:
                            pairs = [(col("ret").rearrange("b (k c) -> b k c", k=3)[:, :, i * P:(i + 1) * P],
                                      Y[0:NB, b, 0:3 * P].rearrange("p (k c) -> p k c", k=3))]
                        for dst, src in pairs:
                            hit(sp.dma_start(dst, src), f"y_out{b}", 16)
                    elif kd == "y" and st.r < T and UNITS[st.u]["kind"] != "ret":
                        unit, r, b = UNITS[st.u], st.r, st.z.b
                        i = unit["i"]
                        sp.wait_ge(S["y_ready"], st.up)
                        rs_ = slice(r * P, (r + 1) * P)
                        if unit["kind"] == "fox":
                            dst = fox_p[bass.ds(l, 1), 0, rs_, :, 2 * i:2 * i + 2, :].rearrange("o p k h d -> (o p) k (h d)")
                            hit(sp.dma_start(dst, Y[:, b, P:3 * P].rearrange("p (k c) -> p k c", k=2)), f"y_out{b}", 16)
                        else:
                            slots = heads(Y[:, b, :])
                            for t_, sl, rr in ((cmp_p, slots[:, 6:8, :], rs_), (slc_p, slots[:, 4:9:4, :], rs_),
                                               (win_p, slots[:, 5:10:4, :], slice((r - WT) * P, (r - WT + 1) * P))):
                                if t_ is win_p and r < T - WT:
                                    continue
                                dst = t_[bass.ds(l, 1), 0, rr, :, i, :].rearrange("o p k d -> (o p) k d")
                                hit(sp.dma_start(dst, sl), f"y_out{b}", 16)
                    elif kd == "logf":
                        sp.wait_ge(S["lf_ready"], st.c)
                        dst = logf_p[bass.ds(l, 1), 0].rearrange("o (t p) h -> p (o t) h", p=P)
                        with nc.allow_non_contiguous_dma(reason="four heads of a row"):
                            hit(sp.dma_start(dst, lf[:, 0, 0:T, :]), "lf_st", 16)
                            hit(sp.dma_start(at_layer(logf_s, "o b t h -> (o b) (t h)"), lf[0:NB, 0, T, :]), "lf_st", 16)
                        sp.wait_ge(S["lf_scan"], st.scan)
                        hit(sp.dma_start(c_d, cT[:]), "c_out", 16)
                    elif kd == "gn":
                        i, b, r = UNITS[st.u]["i"], st.r % 2, st.r
                        sp.wait_ge(S["gn_out"], st.up)
                        c = (HA + HB) * HD + i * P
                        hit(sp.dma_start(mix_d[r * P:(r + 1) * P, c:c + P], ret_mix[:, b, :]), f"mx_out{b}", 16)
                    elif kd == "ret_state":
                        i = UNITS[st.u]["i"]
                        wait(sp, st.o)
                        for h in range(2):
                            hs = slice(h * HD, (h + 1) * HD)
                            hit(sp.dma_start(ret_p[bass.ds(l, 1), 0, 2 * i + h].rearrange("o d e -> (o d) e"), rstate[hs, hs]), "ret_st", 16)
                    elif kd == "OT" and st.it.br in ("slc", "fox"):
                        it = st.it
                        i, b, t = UNITS[it.u]["i"], it.acc % 2, it.t
                        sp.wait_ge(S["att_done"], st.up)
                        if it.br == "slc":
                            hit(sp.dma_start(mix_d[t * P:(t + 1) * P, i * 256:(i + 1) * 256], acc[:, b, :]), f"mix_out{b}", 16)
                        else:
                            c = HA * HD + (2 * i + it.h) * HD
                            dst = mix_d[t * P:(t + 4) * P, c:c + HD].rearrange("(a p) d -> p a d", p=P)
                            hit(sp.dma_start(dst, heads(acc[:, b, :])), f"mix_out{b}", 16)
                    elif kd == "out":
                        def residual(r):
                            if r >= 2:
                                sp.wait_ge(S[f"row_out{r % 2}"], 16 * (r // 2))
                            src = y_prompt[0, r * P:(r + 1) * P, :] if r < T else y_sample[:, 0, :]
                            hit(sp.dma_start(res[0:rows(r), r % 2, :], src), f"res_in{r % 2}", 16)

                        r, n = st.r, rows(st.r)
                        if r == 0:
                            sp.wait_ge(S["pe_z"], st.z.up - 1)
                            residual(0)
                        if r < T:
                            residual(r + 1)
                        wait(sp, st.z.free)
                        dst = y_prompt[0, r * P:(r + 1) * P, :] if r < T else y_sample[:, 0, :]
                        hit(sp.dma_start(dst, res[0:n, r % 2, :]), f"row_out{r % 2}", 16)
                used = [n for n in sorted(fired) if n not in once and n not in kept]
                for n in used:
                    sp.wait_ge(S[n], fired[n])
                sp.wait_ge(S["ends"], 4 * (l + 1))
                sp.sem_inc(S["norm_in"], 1)
                for n in used + ["s_end"]:
                    sp.sem_clear(S[n])
                sp.sem_inc(S["next_layer"], 1)
        for n in total:
            assert n in ("acc_uses",) or fired.get(n, 0) == total[n], (n, total[n], fired.get(n))


def lay_out(inputs):
    a = {k: np.ascontiguousarray(np.asarray(v)) for k, v in inputs.items()}
    names = ("aq akc avc aks avs akw avw ag agate bq bk bv bf bgate cq ck cv cgate").split()
    widths = [HA * HD] + [KV * HD] * 6 + [3 * HA, HA * HD] + [HB * HD] * 3 + [HB, HB * HD] + [HC * HD] * 4
    start = dict(zip(names, np.cumsum([0] + widths)))
    cols = lambda n, c0, w: np.arange(start[n] + c0, start[n] + c0 + w)
    w = a["w_in"].reshape(DEPTH, K, P, -1)
    blocks = []
    for unit in UNITS:
        i = unit["i"]
        if unit["kind"] == "nsa":
            c = [cols("aq", 256 * i, 256), cols("aks", HD * i, HD)]
            if i == 0:
                c += [cols("ag", 0, 3 * HA), cols("bf", 0, HB)]
            c += [cols(n, HD * i, HD) for n in ("akw", "akc", "avc", "avs", "avw")]
        elif unit["kind"] == "gate":
            c = [cols("agate", 0, 512)] if i == 0 else [cols("bgate", 0, 256), cols("cgate", 0, 256)]
        else:
            g = {"fox": "b", "ret": "c"}[unit["kind"]]
            c = [cols(g + n, P * i, P) for n in "qkv"]
        c = np.concatenate(c)
        assert len(c) == unit["width"]
        blocks.append(w[:, :, :, c].transpose(0, 2, 1, 3).reshape(DEPTH, P, -1))
    kn = a["nsa_k_norm"]
    consts, s_consts, rope_new = shape_constants()
    return {
        "x_prompt": a["x_prompt"], "x_sample": a["x_sample"], "cache_cmp": a["cache_nsa_cmp"], "cache_slc": a["cache_nsa_slc"],
        "cache_fox": a["cache_fox_kv"], "cache_logf": a["cache_fox_logf"], "state_win": a["state_nsa_win"],
        "state_ret": a["state_ret"], "page_table": a["page_table"],
        "w_in": np.ascontiguousarray(np.concatenate(blocks, 2)),
        "w_out": np.ascontiguousarray(a["w_out"].reshape(DEPTH, K, P, D).transpose(0, 2, 1, 3)),
        "norm_w": a["norm_w"],
        "w7_in": np.concatenate([a["nsa_q_norm"]] * 4 + [kn[:, 1], kn[:, 2], kn[:, 0]], 1),
        "w4_in": np.concatenate([a["fox_q_norm"]] * 2 + [a["fox_k_norm"]] * 2, 1),
        "gn_w": a["ret_gn_w"], "fox_bf": a["fox_bf"], "consts": consts, "s_consts": s_consts, "rope_new": rope_new}


OUTS = [("y_prompt", (1, SEQ, D)), ("y_sample", (NB, 1, D)),
        ("cmp_p", (DEPTH, 1, SEQ, 2, KV, HD)), ("cmp_s", (DEPTH, NB, 1, 2, KV, HD)),
        ("slc_p", (DEPTH, 1, SEQ, 2, KV, HD)), ("slc_s", (DEPTH, NB, 1, 2, KV, HD)),
        ("fox_p", (DEPTH, 1, SEQ, 2, HB, HD)), ("fox_s", (DEPTH, NB, 1, 2, HB, HD)),
        ("logf_p", (DEPTH, 1, SEQ, HB)), ("logf_s", (DEPTH, NB, 1, HB)),
        ("win_p", (DEPTH, 1, WINDOW, 2, KV, HD)), ("win_s", (DEPTH, NB, WINDOW, 2, KV, HD)),
        ("ret_p", (DEPTH, 1, HC, HD, HD)), ("ret_s", (DEPTH, NB, HC, HD, HD))]


def kernel(**inputs):
    import concourse.bacc as bacc
    from concourse.bass_utils import run_bass_kernel_spmd

    nc = bacc.Bacc("TRN2", target_bir_lowering=False, num_devices=1)
    arrays = {f"in_{n}": v for n, v in lay_out(inputs).items()}
    args = [nc.dram_tensor(n, v.shape, mybir.dt.from_np(v.dtype), kind="ExternalInput").ap() for n, v in arrays.items()]
    args += [nc.dram_tensor(f"out_{n}", shape, F32, kind="ExternalOutput").ap() for n, shape in OUTS]
    decoder_step(nc, *args)
    r = run_bass_kernel_spmd(nc, [arrays], core_ids=[0])
    return tuple(r.results[0][f"out_{n}"] for n, _ in OUTS)
```
